# Optimizing a Trainium2 kernel written in Bass

```python
import math
import jax, jax.numpy as jnp
from jax import lax
import numpy as np

D_MODEL = 1024
BATCH = 1
SEQ = 1024
DEPTH = 2

N_A_LAYERS = DEPTH // 2
N_B_LAYERS = DEPTH - N_A_LAYERS
CHUNK = 128
SGU_WIDTH = 2 * D_MODEL
SGU_GROUPS = 8
HEAD_DIM = 64
KV_HEADS = D_MODEL // 128
DILATED_GROUPS = ((128, 1), (512, 4), (2048, 16))
N_GROUPS = len(DILATED_GROUPS)
Q_HEADS = N_GROUPS * KV_HEADS
BLK = 128
REL_BUCKETS = 32
REL_MAX_DIST = 2048
D_FF = 2816
CONV_WIDTH = 3
ALPHA = (2 * DEPTH) ** 0.25
BETA = (8 * DEPTH) ** -0.25
LN_EPS = 1e-5
NEG = -1e30

kernel_name = 'hybrid_sgu_dilated_yoco'

def layer_norm(x, g, b):
    xf = x.astype(jnp.float32)
    mu = jnp.mean(xf, axis=-1, keepdims=True)
    var = jnp.mean(jnp.square(xf - mu), axis=-1, keepdims=True)
    y = (xf - mu) * lax.rsqrt(var + LN_EPS) * g.astype(jnp.float32) + b.astype(jnp.float32)
    return y.astype(x.dtype)

def conv_ffn(x, w_up, conv_w, conv_b, w_down):
    T = x.shape[1]
    h = x @ w_up
    hp = jnp.pad(h, ((0, 0), (CONV_WIDTH - 1, 0), (0, 0)))
    h = sum(hp[:, k:k + T] * conv_w[k] for k in range(CONV_WIDTH)) + conv_b
    a, g = jnp.split(h, 2, axis=-1)
    return (jax.nn.gelu(a, approximate=False) * g) @ w_down

def mixer_a(x, w_in, ln_g, ln_b, w_s, b_s, w_out):
    B, T, _ = x.shape
    z = jax.nn.gelu(x @ w_in, approximate=False)
    u, v = jnp.split(z, 2, axis=-1)
    v = layer_norm(v, ln_g, ln_b)
    v = v.reshape(B, T // CHUNK, CHUNK, SGU_GROUPS, SGU_WIDTH // SGU_GROUPS)
    ws = w_s * jnp.tril(jnp.ones((CHUNK, CHUNK), w_s.dtype))
    sv = jnp.einsum('gts,bnsgc->bntgc', ws, v) + b_s.T[None, None, :, :, None]
    y = u * sv.reshape(B, T, SGU_WIDTH)
    return y @ w_out

def t5_bucket(dist):
    n = dist.astype(jnp.int32)
    max_exact = REL_BUCKETS // 2
    nf = jnp.maximum(n, 1).astype(jnp.float32)
    large = max_exact + (jnp.log(nf / max_exact) / math.log(REL_MAX_DIST / max_exact)
                         * (REL_BUCKETS - max_exact)).astype(jnp.int32)
    large = jnp.minimum(large, REL_BUCKETS - 1)
    return jnp.where(n < max_exact, n, large)

def band_delta():
    iq = jnp.arange(BLK)[:, None]
    ik = jnp.arange(2 * BLK)[None, :]
    return iq + BLK - ik

def band_bias(table_g, dil):
    dist = jnp.clip(band_delta(), 0, None) * dil
    return jnp.transpose(table_g[t5_bucket(dist)], (2, 0, 1)).astype(jnp.float32)

def dilated_band_attention(q, k, v, dil, n_back, bias):
    B, T, H, Dh = q.shape
    span = dil * BLK
    Tp = -(-T // span) * span
    S = Tp // dil
    NB = S // BLK

    def to_blocks(a):
        a = jnp.pad(a, ((0, 0), (0, Tp - T), (0, 0), (0, 0)))
        a = a.reshape(B, S, dil, H, Dh).transpose(0, 2, 3, 1, 4)
        return a.reshape(B, dil, H, NB, BLK, Dh)

    def band(a):
        prev = jnp.pad(a[:, :, :, :-1], ((0, 0), (0, 0), (0, 0), (1, 0), (0, 0), (0, 0)))
        return jnp.concatenate([prev, a], axis=4)

    qb, kb, vb = to_blocks(q), band(to_blocks(k)), band(to_blocks(v))
    s = jnp.einsum('brhnqd,brhnkd->brhnqk', qb, kb).astype(jnp.float32) * (Dh ** -0.5)
    s = s + bias[:, None]
    delta = band_delta()
    valid = (delta >= 0) & (delta <= n_back)
    first = (jnp.arange(NB)[:, None, None] == 0) & (jnp.arange(2 * BLK)[None, None, :] < BLK)
    valid = valid[None] & ~first
    s = jnp.where(valid, s, NEG)
    m = jnp.max(s, axis=-1, keepdims=True)
    p = jnp.exp(s - m)
    den = jnp.sum(p, axis=-1, keepdims=True)
    o = jnp.einsum('brhnqk,brhnkd->brhnqd', (p / den).astype(v.dtype), vb)
    lse = (m + jnp.log(den))[..., 0]
    o = o.reshape(B, dil, H, S, Dh).transpose(0, 3, 1, 2, 4).reshape(B, Tp, H, Dh)[:, :T]
    lse = lse.reshape(B, dil, H, S).transpose(0, 3, 1, 2).reshape(B, Tp, H)[:, :T]
    return o, lse

def mixer_b(x, k, v, w_q, w_o, rel_table):
    B, T, _ = x.shape
    q = (x @ w_q).reshape(B, T, N_GROUPS, KV_HEADS, HEAD_DIM)
    outs, lses = [], []
    for g, (win, dil) in enumerate(DILATED_GROUPS):
        bias = band_bias(rel_table[:, g * KV_HEADS:(g + 1) * KV_HEADS], dil)
        o, lse = dilated_band_attention(q[:, :, g], k, v, dil, win // dil, bias)
        outs.append(o)
        lses.append(lse)
    wts = jax.nn.softmax(jnp.stack(lses, axis=0), axis=0)
    o = jnp.einsum('gbth,gbthd->bthd', wts, jnp.stack(outs, axis=0).astype(jnp.float32))
    return o.reshape(B, T, KV_HEADS * HEAD_DIM).astype(x.dtype) @ w_o

def setup_inputs(seed: int = 0) -> dict:
    key = jax.random.key(seed)
    ks = jax.random.split(key, 20)
    f32 = jnp.float32
    nrm = lambda k, shape, s: jax.random.normal(k, shape, f32) * s
    E2 = 2 * SGU_WIDTH
    return {
        'x': nrm(ks[0], (BATCH, SEQ, D_MODEL), 1.0),
        'a_w_in': nrm(ks[1], (N_A_LAYERS, D_MODEL, E2), D_MODEL ** -0.5),
        'a_ln_g': 1.0 + nrm(ks[2], (N_A_LAYERS, SGU_WIDTH), 0.05),
        'a_ln_b': nrm(ks[3], (N_A_LAYERS, SGU_WIDTH), 0.02),
        'a_w_s': nrm(ks[4], (N_A_LAYERS, SGU_GROUPS, CHUNK, CHUNK), CHUNK ** -0.5),
        'a_b_s': 1.0 + nrm(ks[5], (N_A_LAYERS, SGU_GROUPS, CHUNK), 0.1),
        'a_w_out': nrm(ks[6], (N_A_LAYERS, SGU_WIDTH, D_MODEL), BETA * SGU_WIDTH ** -0.5),
        'kv_w': nrm(ks[7], (D_MODEL, 2 * KV_HEADS * HEAD_DIM), D_MODEL ** -0.5),
        'b_w_q': nrm(ks[8], (N_B_LAYERS, D_MODEL, Q_HEADS * HEAD_DIM), D_MODEL ** -0.5),
        'b_w_o': nrm(ks[9], (N_B_LAYERS, KV_HEADS * HEAD_DIM, D_MODEL), BETA * (KV_HEADS * HEAD_DIM) ** -0.5),
        'rel_table': nrm(ks[10], (REL_BUCKETS, Q_HEADS), 0.5),
        'ffn_w_up': nrm(ks[11], (DEPTH, D_MODEL, 2 * D_FF), D_MODEL ** -0.5),
        'ffn_conv_w': nrm(ks[12], (DEPTH, CONV_WIDTH, 2 * D_FF), CONV_WIDTH ** -0.5),
        'ffn_conv_b': nrm(ks[13], (DEPTH, 2 * D_FF), 0.02),
        'ffn_w_down': nrm(ks[14], (DEPTH, D_FF, D_MODEL), BETA * D_FF ** -0.5),
        'ln_g': 1.0 + nrm(ks[15], (DEPTH, 2, D_MODEL), 0.05),
        'ln_b': nrm(ks[16], (DEPTH, 2, D_MODEL), 0.02),
    }

def reference(x, a_w_in, a_ln_g, a_ln_b, a_w_s, a_b_s, a_w_out, kv_w, b_w_q, b_w_o,
              rel_table, ffn_w_up, ffn_conv_w, ffn_conv_b, ffn_w_down, ln_g, ln_b):
    B, T, _ = x.shape
    k = v = None
    for i in range(DEPTH):
        if i < N_A_LAYERS:
            h = mixer_a(x, a_w_in[i], a_ln_g[i], a_ln_b[i], a_w_s[i], a_b_s[i], a_w_out[i])
        else:
            if i == N_A_LAYERS:
                kv = (x @ kv_w).reshape(B, T, 2, KV_HEADS, HEAD_DIM)
                k, v = kv[:, :, 0], kv[:, :, 1]
            j = i - N_A_LAYERS
            h = mixer_b(x, k, v, b_w_q[j], b_w_o[j], rel_table)
        x = layer_norm(ALPHA * x + h, ln_g[i, 0], ln_b[i, 0])
        f = conv_ffn(x, ffn_w_up[i], ffn_conv_w[i], ffn_conv_b[i], ffn_w_down[i])
        x = layer_norm(ALPHA * x + f, ln_g[i, 1], ln_b[i, 1])
    return x


_drawn_inputs = setup_inputs


def setup_inputs(seed=0):
    import zlib

    import numpy as np

    out = dict(_drawn_inputs(seed))
    spreads = {}
    factors = {'a_ln_g': 6.662, 'a_ln_b': 26.735, 'ffn_conv_b': 6.044, 'a_b_s': 3.181}
    for name, (base, spread) in spreads.items():
        noise = np.random.default_rng([zlib.crc32(name.encode()), seed]).standard_normal(out[name].shape)
        drawn = base * np.exp(spread * noise) if base else spread * noise
        out[name] = __import__('jax').numpy.asarray(drawn.astype(out[name].dtype))
    for name, factor in factors.items():
        out[name] = (out[name] * factor).astype(out[name].dtype)
    return out
```

```python
from contextlib import ExitStack

import concourse.bass as bass
from concourse import mybir

F32 = mybir.dt.float32
F32R = mybir.dt.float32r
ACT = mybir.ActivationFunctionType
ALU = mybir.AluOpType
ds = bass.ds

P = 128
T = 1024
D = 1024
KT = D // P
TT = T // P
HALF = 512
W_SGU = 2048
CT = W_SGU // P
SG = 8
D_FF = 2816
FT = D_FF // P
FI = FT // 2
HD = 64
NPAIR = 4
DIL = (1, 4, 16)
TABW = 384
ROW = 2 * HD + 4
ALPHA = 4 ** 0.25
EPS = 1e-5
BIG = 1e30
ONE = 1
DMA = 16


def program(nc, x, a_w_in, a_ln_g, a_ln_b, a_w_s, a_b_s, a_w_out, kv_w, b_w_q, b_w_o, rel_table,
            ffn_w_up, ffn_conv_w, ffn_conv_b, ffn_w_down, ln_g, ln_b, bucket_pick, identity, out):
    ctx = ExitStack()
    with ctx:
        def sb(name, shape, dt=F32):
            return ctx.enter_context(nc.sbuf_tensor(name, shape, dt))

        def sem(name):
            return ctx.enter_context(nc.semaphore(name))

        xt_hi = sb("xt_hi", [P, KT, T], F32R)
        xt_lo = sb("xt_lo", [P, KT, T], F32R)
        col_hi = sb("col_hi", [P, 2, KT, P], F32R)
        col_lo = sb("col_lo", [P, 2, KT, P], F32R)
        wide_hi = sb("wide_hi", [P, 2, D], F32R)
        wide_lo = sb("wide_lo", [P, 2, D], F32R)
        hid_hi = sb("hid_hi", [P, 2, T], F32R)
        hid_lo = sb("hid_lo", [P, 2, T], F32R)
        res = sb("res", [P, TT, D])
        raw_col = sb("raw_col", [P, 2, KT, P])
        raw_wide = sb("raw_wide", [P, 2, D])
        par = sb("par", [P, 5, 88])
        ident = sb("ident", [P, P])
        WORK = 11616
        work = sb("work", [P, WORK])

        def view(at, n):
            return work[:, at:at + n]

        tmp = [view(K * T, T) for K in range(4)]
        bias_ts = view(4096, 2048).rearrange("p (c t) -> p c t", c=CT)
        ws_t = view(6144, 1024)
        v_in = [view(7168 + s * 1024, 1024) for s in range(2)]
        bs_rows = view(7168, 1024)
        ones = view(8192, P)
        v_stats = view(9216, TT * 8 * 6).rearrange("p (t j x) -> p t j x", t=TT, j=8)
        gb = view(9216, 2 * D)
        v_mv = view(11264, 2 * TT).rearrange("p (t x) -> p t x", x=2)
        ln_mv = view(11280, 2 * TT).rearrange("p (t x) -> p t x", x=2)
        v_rstd = view(11296, TT)
        ln_rstd = view(11304, TT)
        v_half = view(11312, TT)
        ln_stats = view(11320, TT * 12).rearrange("p (t j x) -> p t j x", t=TT, j=2)
        nat = [view(g * TT * ROW, TT * ROW).rearrange("p (t r) -> p t r", t=TT) for g in range(3)]
        k_t = view(3168, T)
        q_t = [view(4192 + s * T, T) for s in range(2)]
        v_perm = [view(6240 + s * T, T).rearrange("p (t c) -> p t c", t=TT) for s in range(2)]
        b_at = [8288, 8800, 9312]
        b_w = [256, 256, 128]
        bias = [view(b_at[g], 2 * b_w[g]).rearrange("p (h w) -> p h w", h=2) for g in range(3)]
        prob = [view(9568 + s * 512, 512).rearrange("p (h w) -> p h w", h=2) for s in range(2)]
        prob_t = [view(10592 + s * 512, 512).rearrange("p (h w) -> p h w", h=2) for s in range(2)]
        mix = view(9568, 160)
        table = view(9600, 24)
        pick = view(9632, 3 * TABW)
        tab_rows = view(4096, 3 * TABW)

        up = [ctx.enter_context(nc.psum_tensor(f"up{b}", [P, 2 * HALF], F32)) for b in range(2)]
        down = [ctx.enter_context(nc.psum_tensor(f"down{b}", [P, 2 * HALF], F32)) for b in range(2)]

        v_dram = nc.dram_tensor("v_scratch", [CT, P, TT * P], F32).ap()
        vnat_dram = nc.dram_tensor("attn_v_scratch", [T, 4 * P], F32).ap()
        o_dram = nc.dram_tensor("attn_out_scratch", [2, T, ROW], F32).ap()
        tab_dram = nc.dram_tensor("bias_rows_scratch", [24, TABW], F32).ap()
        skew_dram = nc.dram_tensor("bias_skew_scratch", [24, P * TABW], F32).ap()

        ident_in, par_in = sem("ident_in"), sem("par_in")
        ws_in, bs_in, tab_in = sem("ws_in"), sem("bs_in"), sem("tab_in")
        x_in = [sem(f"x_in{s}") for s in range(2)]
        pool_step = sem("pool_step")
        consts_ready = sem("consts_ready")
        tab_stored, skew_stored = sem("tab_stored"), sem("skew_stored")
        ws_masked = sem("ws_masked")
        col_in = [sem(f"col_in{s}") for s in range(2)]
        wide_in = [sem(f"wide_in{s}") for s in range(2)]
        col_hi_done, col_lo_done = sem("col_hi_done"), sem("col_lo_done")
        wide_hi_done, wide_lo_done = sem("wide_hi_done"), sem("wide_lo_done")
        up_done, down_done = sem("up_done"), sem("down_done")
        up_free = [sem(f"up_free{b}") for b in range(2)]
        down_free = [sem(f"down_free{b}") for b in range(2)]
        xt_hi_done, res_scaled = sem("xt_hi_done"), sem("res_scaled")
        v_counted = sem("v_counted")
        v_stored = [sem(f"v_stored{k}") for k in range(4)]
        v_mean, v_scale, v_norm = sem("v_mean"), sem("v_scale"), sem("v_norm")
        v_loaded = [sem(f"v_loaded{s}") for s in range(2)]
        tap0_done, tap1_done, gate_act = sem("tap0_done"), sem("tap1_done"), sem("gate_act")
        y_done, hid_hi_done, hid_ready = sem("y_done"), sem("hid_hi_done"), sem("hid_ready")
        gb_in = sem("gb_in")
        ln_counted, ln_mean, ln_scale = sem("ln_counted"), sem("ln_mean"), sem("ln_scale")
        ln_step, xn_done = sem("ln_step"), sem("xn_done")
        out_stored = [sem(f"out_stored{s}") for s in range(2)]
        attn_v_stored = sem("attn_v_stored")
        logits_a, exp_done, turned, prob_t_ready = sem("logits_a"), sem("exp_done"), sem("turned"), sem("prob_t_ready")
        vp_in = [sem(f"vp_in{g}") for g in range(3)]
        bias_in = [sem(f"bias_in{g}") for g in range(3)]
        bias_clear = sem("bias_clear")
        nat_stored = [None, sem("nat_stored1"), sem("nat_stored2")]
        nat_in = [None, sem("nat_in1"), sem("nat_in2")]
        mix_step, mix_delta, mix_exp = sem("mix_step"), sem("mix_delta"), sem("mix_exp")
        o_done, o_hi_done = sem("o_done"), sem("o_hi_done")

        class Base:
            def __init__(self, col, wide, in0, up, in1=0, down=0, hid=0, tap=0):
                self.col, self.wide, self.in0, self.in1 = col, wide, in0, in1
                self.up, self.down, self.hid, self.tap = up, down, hid, tap

        X_UP = 0
        SET_UP = X_UP + TT
        DOWN0 = TT
        V1 = Base(col=0, wide=0, in0=0, in1=0, up=SET_UP + 6)
        G1 = Base(col=8, wide=8, in0=4, in1=4, up=V1.up + 16, down=DOWN0, hid=0)
        LN_UP = [G1.up + 4 * SG]
        F1 = Base(col=G1.col + 2 * SG, wide=G1.wide + 2 * SG, in0=G1.in0 + SG, in1=G1.in1 + SG, up=LN_UP[0] + TT,
                  down=G1.down + TT * SG, hid=2 * SG, tap=0)
        LN_UP.append(F1.up + 4 * FI)
        V2 = Base(col=F1.col + 4 * FI, wide=F1.wide + 2 * FI, in0=F1.in0 + FI, in1=F1.in1 + FI, up=LN_UP[1] + TT,
                  down=F1.down + TT * FI)
        PAIR_UP, PAIR_DOWN = 30, 24 + TT
        AT = Base(col=V2.col + 2, wide=V2.wide + 2, in0=V2.in0 + 1, up=V2.up + 4, down=V2.down)
        LN_UP.append(AT.up + NPAIR * PAIR_UP)
        F2 = Base(col=AT.col + 4 * NPAIR, wide=AT.wide + NPAIR, in0=AT.in0 + NPAIR, in1=V2.in1 + 1,
                  up=LN_UP[2] + TT, down=AT.down + NPAIR * PAIR_DOWN, hid=F1.hid + 2 * FI, tap=4 * FI)
        STEP_UP = {2: 3, 1: 12, 0: 20}
        Q0_UP, TURN_UP = 11, 28
        STEP_DOWN = {2: 0, 1: 8, 0: 16}

        def freed(base, j, more=0):
            return base // 2 + j + 2 + more

        def wait_apart(eng, *waits):
            waits = [(to, eng.to_reg(value)) for to, value in waits]
            eng.wait_ge(consts_ready, 2)
            for to, value in waits:
                eng.wait_ge(to, value)

        def wait_turned(eng, n):
            at = X_UP if n == 0 else LN_UP[n - 1]
            for b in range(2):
                eng.wait_ge(up_free[b], freed(at, TT // 2 - 1))

        def wait_added(eng, down_end):
            for b in range(2):
                eng.wait_ge(down_free[b], down_end // 2 + 1)

        def col_piece(w, at, i, step):
            n = w.shape[1] // (step * P)
            v = w.rearrange("(k p) (i s n) -> i s p k n", p=P, s=step, n=P)
            return v[ds(i, 1), at].rearrange("a p k n -> (a p) k n")

        def row_piece(w, at, i, step):
            v = w.rearrange("(i s p) n -> i s p n", s=step, p=P)
            return v[ds(i, 1), at].rearrange("a p n -> (a p) n")

        w_u, w_v = a_w_in[0][:, 0:W_SGU], a_w_in[0][:, W_SGU:2 * W_SGU]
        w_out, w_q, w_o = a_w_out[0], b_w_q[0], b_w_o[0]
        w_k, w_kv = kv_w[:, 0:4 * P], kv_w[:, 4 * P:8 * P]
        xt_hi_t = xt_hi[:].rearrange("p k (i s t) -> p k i s t", s=2, t=P)
        xt_lo_t = xt_lo[:].rearrange("p k (i s t) -> p k i s t", s=2, t=P)
        res_t = res[:].rearrange("p (i s) d -> p i s d", s=2)
        wide_k_hi = wide_hi[:].rearrange("p s (k n) -> p s k n", n=P)
        wide_k_lo = wide_lo[:].rearrange("p s (k n) -> p s k n", n=P)
        conv = par[:, 0:4, :].rearrange("p (l b) (j g i s) -> p l b j g i s", l=2, j=2, g=2, s=2)

        def tap(l, k, q, i):
            return conv[:, l, k // 2, k % 2, q // 2, ds(i, 1), q % 2]

        def tok_tile(a, i, s):
            return a[:, :, ds(i, 1), s].rearrange("p k a t -> p k (a t)")

        def res_tile(i, s):
            return res_t[:, ds(i, 1), s].rearrange("p a d -> p (a d)")

        def steps(g):
            first = {0: [k == 0 for k in range(8)], 1: [k % 2 == 0 for k in range(8)], 2: [True] * 8}[g]
            return [(k, [k] if first[k] else [k - 1, k], P if first[k] else 2 * P) for k in range(8)]

        def tokens(a, g, t, n):
            if g == 0:
                return a[:, (t + 1 - n) * P:(t + 1) * P]
            if g == 1:
                v = a.rearrange("p (s r) -> p r s", r=4)[:, t // 2]
                return v if n == 2 else v[:, (t % 2) * P:(t % 2 + 1) * P]
            return a.rearrange("p (s t h) -> p t h s", t=8, h=2)[:, t]

        block = ctx.enter_context(nc.Block())

        @block.sync
        def _(sp):
            for s in range(2):
                sp.sem_inc(out_stored[s], DMA)

            def col_load(B, j, s, src):
                sp.wait_ge(col_lo_done, B.col + 2 * j + s + 1)
                sp.dma_start(raw_col[:, s], src).then_inc(col_in[s], DMA)

            def wide_load(B, j, s, src):
                sp.wait_ge(wide_lo_done, B.wide + 2 * j + s + 1)
                sp.dma_start(raw_wide[:, s], src).then_inc(wide_in[s], DMA)

            def wide_col_load(B, j, s, src):
                sp.wait_ge(wide_lo_done, B.wide + 2 * j + s + 1)
                sp.dma_start(raw_wide[:, s].rearrange("p (k n) -> p k n", n=P), src).then_inc(wide_in[s], DMA)

            sp.dma_start(ident[:], identity).then_inc(ident_in, DMA)
            with sp.Fori(0, TT // 2) as i:
                for s in range(2):
                    sp.wait_ge(res_scaled, 2 * i + s + 1)
                    sp.dma_start(tmp[s], row_piece(x[0], s, i, 2)).then_inc(x_in[s], DMA)
            rows = tmp[2]
            for l in range(2):
                for k in range(4):
                    src = ffn_conv_w[l, k:k + 1] if k < 3 else ffn_conv_b[l:l + 1]
                    sp.dma_start(rows[44 * (k % 2):44 * (k % 2) + 44, (2 * l + k // 2) * P:(2 * l + k // 2 + 1) * P],
                                 src.rearrange("a (r n) -> (a r) n", n=P)).then_inc(par_in, DMA)
            for k, src in enumerate((a_ln_g, a_ln_b)):
                sp.dma_start(rows[CT * k:CT * (k + 1), 4 * P:5 * P],
                             src.rearrange("a (r n) -> (a r) n", n=P)).then_inc(par_in, DMA)
            sp.wait_ge(consts_ready, 1)
            sp.dma_start(table[0:32, :], rel_table).then_inc(tab_in, DMA)
            sp.dma_start(pick[0:33, :], bucket_pick).then_inc(tab_in, DMA)
            sp.dma_start(ws_t.rearrange("p (g s) -> p g s", g=SG), a_w_s[0].rearrange("g t s -> t g s")).then_inc(ws_in, DMA)
            sp.dma_start(bs_rows, a_b_s.rearrange("a g t -> a (g t)").to_broadcast([P, SG * P])).then_inc(bs_in, DMA)
            with sp.Fori(0, 4) as i:
                for k in range(2):
                    col_load(V1, i, k, col_piece(w_v, k, i, 4))
                for k in range(2):
                    wide_col_load(V1, i, k, col_piece(w_v, 2 + k, i, 4))
            with sp.Fori(0, SG) as i:
                for s in range(2):
                    col_load(G1, i, s, col_piece(w_u, s, i, 2))
                for k in range(2):
                    wide_load(G1, i, k, row_piece(w_out, k, i, 2))

            def ffn_loads(l, B):
                wu, wd = ffn_w_up[l], ffn_w_down[l]
                with sp.Fori(0, FI) as i:
                    for q in range(4):
                        half = wu[:, (q // 2) * D_FF:(q // 2 + 1) * D_FF]
                        col_load(B, 2 * i + q // 2, q % 2, col_piece(half, q % 2, i, 2))
                        if q % 2:
                            wide_load(B, i, q // 2, row_piece(wd, q // 2, i, 2))

            ffn_loads(0, F1)
            with sp.Fori(0, 1) as i:
                for k in range(2):
                    col_load(V2, i, k, col_piece(w_kv, k, i, 4))
                for k in range(2):
                    wide_col_load(V2, i, k, col_piece(w_kv, 2 + k, i, 4))
            with sp.Fori(0, NPAIR) as i:
                for q, src in enumerate((w_k, w_q[:, 8 * P:12 * P], w_q[:, 4 * P:8 * P], w_q[:, 0:4 * P])):
                    col_load(AT, 2 * i + q // 2, q % 2, col_piece(src, 0, i, 1))
                sp.wait_ge(wide_lo_done, AT.wide + i + 2)
                sp.dma_start(raw_wide[:, 0], row_piece(w_o, 0, i, 1)).then_inc(wide_in[0], DMA)
            sp.wait_ge(wide_lo_done, F2.wide + 2)
            ffn_loads(1, F2)
            out_v = out[0].rearrange("(i s p) n -> i s p n", s=2, p=P)
            with sp.Fori(0, TT // 2) as i:
                for s in range(2):
                    sp.wait_ge(xn_done, 3 * TT + 2 * i + s + 1)
                    sp.dma_start(out_v[ds(i, 1), s].rearrange("a p n -> (a p) n"), tmp[s]).then_inc(out_stored[s], DMA)
            for s in range(2):
                sp.wait_ge(out_stored[s], DMA * (TT // 2 + 1))

        @block.gpsimd
        def _(pool):
            nc.gpsimd.memset(table[0:33, :], BIG).then_inc(consts_ready, ONE)
            nc.gpsimd.memset(ones, 1.0).then_inc(consts_ready, ONE)
            nc.gpsimd.memset(v_half, -0.5).then_inc(pool_step, ONE)
            pool.wait_ge(ws_in, DMA)
            wv = ws_t.rearrange("p (g s) -> p g s", g=SG)
            nc.gpsimd.affine_select(out=wv, in_=wv, compare_op=ALU.is_ge, fill=0.0, base=0,
                                    pattern=[[0, SG], [-1, P]], channel_multiplier=1).then_inc(ws_masked, ONE)
            for b in range(2):
                pool.wait_ge(up_free[b], freed(SET_UP, 1))
            for g in range(3):
                pool.dma_start(tab_dram[8 * g:8 * g + 8], tab_rows[0:8, g * TABW:(g + 1) * TABW]).then_inc(tab_stored, DMA)
            pool.wait_ge(tab_stored, 3 * DMA)
            for g in range(3):
                src = bass.AP(tensor=tab_dram.tensor, offset=8 * g * TABW, ap=[[TABW, 8], [0, P], [1, TABW]])
                pool.dma_start(skew_dram[8 * g:8 * g + 8].rearrange("h (p w) -> h p w", w=TABW), src).then_inc(skew_stored, DMA)
            vd = v_dram.rearrange("(i u c) p (q t n) -> i u c q p t n", u=2, c=2, q=2, t=4)
            with pool.Fori(0, 4) as i:
                for k in range(4):
                    u, q = k // 2, k % 2
                    wait_apart(pool, (up_free[q], freed(V1.up, u) + 2 * i))
                    for c in range(2):
                        pool.dma_start(vd[ds(i, 1), u, c, q].rearrange("a p t n -> (a p) t n"),
                                       tmp[k].rearrange("p (t c n) -> p t c n", t=4, c=2)[:, :, c, :]
                                       ).then_inc(v_stored[k], DMA)
            pool.wait_ge(v_mean, TT)
            nc.gpsimd.tensor_scalar(v_rstd, v_mv[:, :, 1], EPS, None, ALU.add).then_inc(pool_step, ONE)
            pool.wait_ge(pool_step, 2)
            nc.gpsimd.tensor_tensor(v_rstd, v_rstd, v_half, ALU.pow).then_inc(v_scale, ONE)
            for k in range(4):
                pool.wait_ge(v_stored[k], 8 * DMA)
            vl = v_dram.rearrange("(i s) p n -> i s p n", s=2)
            pool.wait_ge(up_free[1], freed(SET_UP, 2))
            with pool.Fori(0, SG) as i:
                for s in range(2):
                    wait_apart(pool, (up_done, G1.up + 4 * i - 2 + 2 * s))
                    pool.dma_start(v_in[s], vl[ds(i, 1), s].rearrange("a p n -> (a p) n")).then_inc(v_loaded[s], DMA)

            def norm_constants(n):
                for k, src in enumerate((ln_g, ln_b)):
                    pool.dma_start(gb[:, k * D:(k + 1) * D],
                                   src[n // 2, n % 2:n % 2 + 1].to_broadcast([P, D])).then_inc(gb_in, DMA)
                pool.wait_ge(ln_mean, TT * (n + 1))
                nc.gpsimd.tensor_scalar(ln_rstd, ln_mv[:, :, 1], EPS, None, ALU.add).then_inc(pool_step, ONE)
                nc.gpsimd.memset(v_half, -0.5).then_inc(pool_step, ONE)
                pool.wait_ge(pool_step, 2 * n + 4)
                nc.gpsimd.tensor_tensor(ln_rstd, ln_rstd, v_half, ALU.pow).then_inc(ln_scale, ONE)

            norm_constants(0)
            wait_turned(pool, 1)
            norm_constants(1)
            wait_turned(pool, 2)
            nc.gpsimd.memset(bias[2], BIG).then_inc(bias_clear, ONE)
            for k in range(4):
                pool.wait_ge(up_free[k % 2], freed(V2.up, k // 2))
                u, q = k // 2, k % 2
                dst = vnat_dram.rearrange("(q t p) (u n) -> q u p t n", q=2, t=4, u=2)[q, u]
                pool.dma_start(dst, tmp[k].rearrange("p (t n) -> p t n", t=4)).then_inc(attn_v_stored, DMA)
            pool.wait_ge(attn_v_stored, 4 * DMA)
            pool.wait_ge(bias_clear, 1)
            pool.wait_ge(skew_stored, 3 * DMA)
            v_tok = [vnat_dram.rearrange("(t p) (i c) -> i p t c", p=P, i=NPAIR),
                     vnat_dram.rearrange("(n p r) (i c) -> i r p n c", n=2, r=4, i=NPAIR),
                     vnat_dram.rearrange("(s t h) (i c) -> i h s t c", s=HD, h=2, i=NPAIR)]
            o_tok = [None, o_dram[0].rearrange("(n p r) c -> r p n c", n=2, r=4),
                     o_dram[1].rearrange("(s t h) c -> h s t c", s=HD, h=2)]

            def skewed(g, hh, at, n, w, i):
                sk = skew_dram[8 * g:8 * g + 8].rearrange("(i h) n -> i h n", h=2)[:, hh]
                v = sk[:, at:at + n * (TABW - 1)].rearrange("i (p w) -> i p w", w=TABW - 1)[:, :, 0:w]
                return v[ds(i, 1)].rearrange("a p w -> (a p) w")

            with pool.Fori(0, NPAIR) as i:
                d = AT.down + PAIR_DOWN * i
                wait_apart(pool, (down_done, d))
                for h in range(2):
                    pool.dma_start(v_perm[0][h * HD:(h + 1) * HD],
                                   v_tok[2][ds(i, 1), h].rearrange("a s t c -> (a s) t c")).then_inc(vp_in[2], DMA)
                for hh in range(2):
                    for h in range(2):
                        pool.dma_start(bias[2][h * HD:(h + 1) * HD, hh, h * HD:(h + 1) * HD],
                                       skewed(2, hh, 255, HD, HD, i)).then_inc(bias_in[2], DMA)
                for hh in range(2):
                    pool.dma_start(bias[1][:, hh], skewed(1, hh, 127, P, 256, i)).then_inc(bias_in[1], DMA)
                for r in range(4):
                    pool.dma_start(v_perm[1][:, 2 * r:2 * r + 2],
                                   v_tok[1][ds(i, 1), r].rearrange("a p n c -> (a p) n c")).then_inc(vp_in[1], DMA)
                for hh in range(2):
                    pool.dma_start(bias[0][:, hh], skewed(0, hh, 127, P, 256, i)).then_inc(bias_in[0], DMA)
                wait_apart(pool, (down_done, d + 8))
                pool.dma_start(v_perm[0], v_tok[0][ds(i, 1)].rearrange("a p t c -> (a p) t c")).then_inc(vp_in[0], DMA)
                for g in (2, 1):
                    wait_apart(pool, *[(down_free[b], freed(AT.down + STEP_DOWN[g], 3) + PAIR_DOWN // 2 * i) for b in range(2)])
                    if g == 2:
                        for h in range(2):
                            pool.dma_start(o_tok[2][h], nat[2][h * HD:(h + 1) * HD]).then_inc(nat_stored[2], DMA)
                    else:
                        for r in range(4):
                            pool.dma_start(o_tok[1][r], nat[1][:, 2 * r:2 * r + 2]).then_inc(nat_stored[1], DMA)
                    stores = 2 if g == 2 else 4
                    wait_apart(pool, (nat_stored[g], stores * DMA * i + stores * DMA))
                    pool.dma_start(nat[g], o_dram[g - 1].rearrange("(t p) c -> p t c", p=P)).then_inc(nat_in[g], DMA)
            pool.wait_ge(o_done, NPAIR)
            norm_constants(2)
            wait_turned(pool, 3)
            norm_constants(3)

        @block.scalar
        def _(act):
            act.sem_inc(res_scaled, 2)

            def hi_col(B, j, s, fills):
                act.wait_ge(col_in[s], DMA * (B.col // 2 + 1) + DMA * j)
                act.wait_ge(up_done, fills)
                nc.scalar.activation(col_hi[:, s], raw_col[:, s], ACT.Copy).then_inc(col_hi_done, ONE)

            def hi_wide(came, j, k, downs=None, fills=None):
                act.wait_ge(wide_in[k], DMA * (came + 1) + DMA * j)
                if downs is not None:
                    act.wait_ge(down_done, downs)
                if fills is not None:
                    act.wait_ge(up_done, fills)
                nc.scalar.activation(wide_hi[:, k], raw_wide[:, k], ACT.Copy).then_inc(wide_hi_done, ONE)

            def turn_in(at, i):
                for s in range(2):
                    act.wait_ge(up_done, at + 2 * i + s + 1)
                    nc.scalar.activation(tok_tile(xt_hi_t, i, s), up[s][:].rearrange("p (k t) -> p k t", k=KT),
                                         ACT.Copy).then_inc(xt_hi_done, ONE)
                    nc.scalar.mul(res_tile(i, s), tmp[s], ALPHA).then_inc(res_scaled, ONE)

            with act.Fori(0, TT // 2) as i:
                turn_in(X_UP, i)
            act.wait_ge(up_done, SET_UP + 1)
            nc.scalar.copy(par[:, 0:4], up[0][:, 0:4 * P].rearrange("p (b n) -> p b n", b=4)[:, :, 0:88]).then_inc(up_free[0], ONE)
            act.wait_ge(up_done, SET_UP + 2)
            nc.scalar.copy(par[:, 4, 0:32], up[1][:, 0:32]).then_inc(up_free[1], ONE)
            act.wait_ge(up_done, SET_UP + 3)
            nc.scalar.copy(tab_rows[0:8, 0:2 * TABW].rearrange("p (g n) -> p g n", g=2),
                           up[0][0:8].rearrange("p (g n) -> p g n", g=2)[:, :, 0:TABW]).then_inc(up_free[0], ONE)
            act.wait_ge(up_done, SET_UP + 4)
            nc.scalar.copy(tab_rows[0:8, 2 * TABW:], up[1][0:8, 0:TABW]).then_inc(up_free[1], ONE)
            act.wait_ge(up_done, SET_UP + 5)
            nc.scalar.copy(ws_t, up[0][:]).then_inc(up_free[0], ONE)

            def v_tiles(i, u, first):
                for q in range(2):
                    k = 2 * u + q
                    act.wait_ge(up_done, V1.up + 4 * i + k + 1)
                    act.wait_ge(v_counted, 4 * i + k + 1)
                    if not first:
                        act.wait_ge(v_stored[k], 2 * DMA * i)
                    nc.scalar.activation(tmp[k], up[q][:], ACT.Gelu).then_inc(up_free[q], ONE)

            for s in range(2):
                hi_col(V1, 0, s, V1.up)
            for start, end in ((0, 1), (1, 4)):
                with act.Fori(start, end) as i:
                    for k in range(2):
                        hi_wide(V1.in0, i, k, fills=V1.up + 4 * i)
                    v_tiles(i, 0, start == 0)
                    for s in range(2):
                        hi_col(V1, i + 1, s, V1.up + 4 * i + 2)
                    v_tiles(i, 1, start == 0)

            def hid_hi_part(B, i, s):
                act.wait_ge(y_done, B.hid + 2 * i + s + 3)
                act.wait_ge(down_done, B.down + TT * i)
                nc.scalar.activation(hid_hi[:, s], tmp[2 + s], ACT.Copy).then_inc(hid_hi_done, ONE)

            for k in range(4):
                act.wait_ge(v_stored[k], 8 * DMA)
            with act.Fori(0, SG) as i:
                for s in range(2):
                    act.wait_ge(up_done, G1.up + 4 * i + 2 * s + 1)
                    act.wait_ge(y_done, G1.hid + 2 * i + s + 1)
                    nc.scalar.activation(tmp[s], up[0][:], ACT.Gelu).then_inc(up_free[0], ONE)
                    hi_col(G1, i + 1, s, G1.up + 4 * i + 2 * s + 1)
                    if s == 0:
                        for k in range(2):
                            hi_wide(G1.in0, i, k, downs=G1.down + TT * i)
                    hid_hi_part(G1, i, s)

            def ln_out(n):
                with act.Fori(0, TT // 2) as i:
                    turn_in(LN_UP[n], i)

            def ffn(l, B):
                def first_tap(i, q):
                    act.wait_ge(up_done, B.up + 4 * i + q + 1)
                    if q < 2:
                        act.wait_ge(y_done, B.hid + 2 * i + q + 1)
                    else:
                        act.wait_ge(hid_ready, B.hid + 2 * i + q - 2 - 1)
                    nc.scalar.activation(tmp[q], up[q % 2][:], ACT.Identity, bias=tap(l, 3, q, i),
                                         scale=tap(l, 2, q, i)).then_inc(tap0_done, ONE)

                def chunk(i, split_next):
                    for q in range(4):
                        if q < 2 or split_next:
                            hi_col(B, 2 * i + 1 + q // 2, q % 2, B.up + 4 * i + q + 1)
                        first_tap(i, q)
                        if q < 2:
                            act.wait_ge(up_free[q], freed(B.up, 2 * i))
                            nc.scalar.activation(tmp[q], tmp[q], ACT.Gelu).then_inc(gate_act, ONE)
                        else:
                            hid_hi_part(B, i, q - 2)
                        if q == 1:
                            for k in range(2):
                                hi_wide(B.in0 if k == 0 else B.in1, i, k, downs=B.down + TT * i)

                with act.Fori(0, FI - 1) as i:
                    chunk(i, True)
                with act.Fori(FI - 1, FI) as i:
                    chunk(i, l == 0)

            ln_out(0)
            ffn(0, F1)
            ln_out(1)
            act.wait_ge(res_scaled, 3 * TT + 2)
            for k in range(2):
                hi_wide(V2.in0 if k == 0 else V2.in1, 0, k, downs=V2.down)
            for k in range(4):
                act.wait_ge(up_done, V2.up + k + 1)
                nc.scalar.copy(tmp[k], up[k % 2][:]).then_inc(up_free[k % 2], ONE)
                if k == 1:
                    for s in range(2):
                        hi_col(AT, 0, s, V2.up + 2)
            act.wait_ge(attn_v_stored, 4 * DMA)
            with act.Fori(0, NPAIR) as i:
                m = AT.up + PAIR_UP * i
                m2 = PAIR_UP // 2 * i
                act.wait_ge(up_done, m + 1)
                nc.scalar.copy(k_t, up[0][:]).then_inc(up_free[0], ONE)
                hi_col(AT, 2 * i + 1, 0, m + 1)
                act.wait_ge(up_done, m + 2)
                nc.scalar.mul(q_t[0].rearrange("p (t h s) -> p t h s", t=8, h=2),
                              up[1][:].rearrange("p (s t h) -> p t h s", t=8, h=2), -HD ** -0.5).then_inc(up_free[1], ONE)
                hi_col(AT, 2 * i + 1, 1, m + 2)
                act.wait_ge(up_done, m + 3)
                nc.scalar.mul(q_t[1], up[0][:], -HD ** -0.5).then_inc(up_free[0], ONE)
                act.wait_ge(wide_in[0], DMA * (AT.in0 + 1) + DMA * i)
                nc.scalar.activation(wide_hi[:, 0], raw_wide[:, 0], ACT.Copy).then_inc(wide_hi_done, ONE)
                hi_col(AT, 2 * i + 2, 0, m + 3)
                for g in (2, 1, 0):
                    if g == 1:
                        act.wait_ge(up_done, m + Q0_UP + 1)
                        nc.scalar.mul(q_t[0], up[1][:], -HD ** -0.5).then_inc(up_free[1], ONE)
                        hi_col(AT, 2 * i + 2, 1, m + Q0_UP + 1)
                    st = steps(g)
                    for k in range(8 + 2):
                        if k < 8:
                            t, keys, w = st[k]
                            b = (STEP_UP[g] + k) % 2
                            for h in range(2):
                                if h == 0:
                                    act.wait_ge(logits_a, 24 * i + STEP_DOWN[g] + k + 1)
                                else:
                                    act.wait_ge(up_free[b], freed(AT.up + STEP_UP[g] + k - b, 0) + m2)
                                e = nc.scalar.activation(prob[k % 2][:, h, 0:w], prob[k % 2][:, h, 0:w], ACT.Exp, scale=-1.0,
                                                         bias=nat[g][:, k, 2 * HD + h:2 * HD + h + 1],
                                                         accum_out=nat[g][:, k, 2 * HD + 2 + h:2 * HD + 3 + h])
                            e.then_inc(exp_done, ONE)
                        if k >= 2:
                            j = k - 2
                            act.wait_ge(down_done, AT.down + PAIR_DOWN * i + STEP_DOWN[g] + j + 1)
                            nc.scalar.copy(nat[g][:, j, 0:2 * HD], down[j % 2][:, HALF:HALF + 2 * HD]).then_inc(down_free[j % 2], ONE)
                act.wait_ge(mix_delta, i + 1)
                nc.scalar.activation(mix[:, 16:64], mix[:, 16:64], ACT.Exp).then_inc(mix_exp, ONE)
                for b in range(2):
                    act.wait_ge(up_done, m + TURN_UP + b + 1)
                    act.wait_ge(down_done, AT.down + PAIR_DOWN * i)
                    nc.scalar.activation(hid_hi[:, 0, b * HALF:(b + 1) * HALF], up[b][:, 0:HALF], ACT.Copy).then_inc(o_hi_done, ONE)
            ln_out(2)
            ffn(1, F2)

        @block.vector
        def _(dve):
            dve.sem_inc(col_lo_done, 2)
            dve.sem_inc(wide_lo_done, 2)
            dve.sem_inc(v_counted, 4)
            dve.sem_inc(y_done, 2)

            def lo_col(B, j, s):
                dve.wait_ge(col_hi_done, B.col + 2 * j + s + 1)
                nc.vector.tensor_tensor(col_lo[:, s], raw_col[:, s], col_hi[:, s], ALU.subtract).then_inc(col_lo_done, ONE)

            def lo_wide(n, k):
                dve.wait_ge(wide_hi_done, n + 1)
                nc.vector.tensor_tensor(wide_lo[:, k], raw_wide[:, k], wide_hi[:, k], ALU.subtract).then_inc(wide_lo_done, ONE)

            def turn_in(n, i, s):
                dve.wait_ge(xt_hi_done, TT * n + 2 * i + s + 1)
                nc.vector.tensor_tensor(tok_tile(xt_lo_t, i, s), up[s][:].rearrange("p (k t) -> p k t", k=KT),
                                        tok_tile(xt_hi_t, i, s), ALU.subtract).then_inc(up_free[s], ONE)

            def add_down(at):
                for t in range(TT):
                    dve.wait_ge(down_done, at + t + 1)
                    nc.vector.tensor_tensor(res[:, t], down[t % 2][:], res[:, t], ALU.add).then_inc(down_free[t % 2], ONE)

            with dve.Fori(0, TT // 2) as i:
                for s in range(2):
                    turn_in(0, i, s)
            dve.wait_ge(bs_in, DMA)
            dve.wait_ge(tab_stored, 3 * DMA)
            dve.wait_ge(up_free[1], freed(SET_UP, 0))
            dve.wait_ge(up_done, SET_UP + 6)
            for c in range(CT):
                g = c // 2
                last = nc.vector.scalar_tensor_tensor(out=bias_ts[:, c], in0=up[1][:, g * P:(g + 1) * P],
                                                      scalar=par[:, 4, CT + c:CT + c + 1], in1=bs_rows[:, g * P:(g + 1) * P],
                                                      op0=ALU.mult, op1=ALU.add)
            last.then_inc(up_free[1], ONE)

            def count_v(i, u):
                for q in range(2):
                    dve.wait_ge(up_free[q], freed(V1.up, u) + 2 * i)
                    for t in range(4):
                        last = nc.vector.bn_stats(v_stats.rearrange("p t (i u) x -> p t i u x", u=2)[:, 4 * q + t, ds(i, 1), u]
                                                  .rearrange("p a x -> p (a x)"),
                                                  tmp[2 * u + q][:, t * 2 * P:(t + 1) * 2 * P])
                    last.then_inc(v_counted, ONE)

            for s in range(2):
                lo_col(V1, 0, s)
            with dve.Fori(0, 4) as i:
                for k in range(2):
                    lo_wide(V1.wide + 2 * i + k, k)
                count_v(i, 0)
                for s in range(2):
                    lo_col(V1, i + 1, s)
                count_v(i, 1)
            dve.wait_ge(v_counted, 4 + 16)
            for t in range(TT):
                nc.vector.bn_aggr(v_mv[:, t], v_stats[:, t].rearrange("p j x -> p (j x)")).then_inc(v_mean, ONE)

            def hid_lo_part(B, i, s):
                dve.wait_ge(hid_hi_done, B.hid + 2 * i + s + 1)
                nc.vector.tensor_tensor(hid_lo[:, s], tmp[2 + s], hid_hi[:, s], ALU.subtract).then_inc(hid_ready, ONE)

            dve.wait_ge(v_scale, 1)
            dve.wait_ge(v_mean, TT)
            with dve.Fori(0, SG) as i:
                for s in range(2):
                    dve.wait_ge(v_loaded[s], DMA * i + DMA)
                    for t in range(TT):
                        last = nc.vector.tensor_scalar(v_in[s][:, t * P:(t + 1) * P], v_in[s][:, t * P:(t + 1) * P],
                                                       v_mv[:, t, 0:1], v_rstd[:, t:t + 1], ALU.subtract, ALU.mult)
                    last.then_inc(v_norm, ONE)
                for s in range(2):
                    lo_col(G1, i + 1, s)
                    if s == 0:
                        for k in range(2):
                            lo_wide(G1.wide + 2 * i + k, k)
                    dve.wait_ge(up_done, G1.up + 4 * i + 2 * s + 2)
                    gain = par[:, 4, 0:CT].rearrange("p (i s) -> p i s", s=2)[:, ds(i, 1), s]
                    term = bias_ts.rearrange("p (i s) t -> p i s t", s=2)[:, ds(i, 1), s].to_broadcast([P, TT, P])
                    nc.vector.scalar_tensor_tensor(out=tmp[2 + s].rearrange("p (t n) -> p t n", t=TT),
                                                   in0=up[1][:].rearrange("p (t n) -> p t n", t=TT), scalar=gain,
                                                   in1=term, op0=ALU.mult, op1=ALU.add).then_inc(up_free[1], ONE)
                    dve.wait_ge(up_free[1], freed(G1.up, s) + 2 * i)
                    dve.wait_ge(up_free[0], freed(G1.up, s) + 2 * i)
                    nc.vector.tensor_tensor(tmp[2 + s], tmp[2 + s], tmp[s], ALU.mult).then_inc(y_done, ONE)
                    hid_lo_part(G1, i, s)
                add_down(G1.down + TT * i)

            def layer_norm(n, turn):
                wait_added(dve, [F1.down, V2.down, F2.down, F2.down + TT * FI][n])
                for t in range(TT):
                    for j in range(2):
                        last = nc.vector.bn_stats(ln_stats[:, t, j], res[:, t, j * HALF:(j + 1) * HALF])
                    last.then_inc(ln_counted, ONE)
                dve.wait_ge(ln_counted, TT * (n + 1))
                for t in range(TT):
                    nc.vector.bn_aggr(ln_mv[:, t], ln_stats[:, t].rearrange("p j x -> p (j x)")).then_inc(ln_mean, ONE)
                dve.wait_ge(ln_mean, TT * (n + 1))
                dve.wait_ge(ln_scale, n + 1)
                dve.wait_ge(gb_in, 2 * DMA * (n + 1))
                mv = ln_mv.rearrange("p (i s) x -> p i s x", s=2)
                rs = ln_rstd.rearrange("p (i s) -> p i s", s=2)
                with dve.Fori(0, TT // 2) as i:
                    for s in range(2):
                        if turn:
                            dve.wait_ge(res_scaled, TT * (n + 1) + 2 * i + s + 1)
                        else:
                            dve.wait_ge(out_stored[s], DMA * i + DMA)
                        nc.vector.tensor_scalar(tmp[s], res_tile(i, s), mv[:, ds(i, 1), s, 0], rs[:, ds(i, 1), s],
                                                ALU.subtract, ALU.mult).then_inc(ln_step, ONE)
                    for s in range(2):
                        dve.wait_ge(ln_step, 4 * (4 * n) + 4 * i + s + 1)
                        nc.vector.tensor_tensor(tmp[s], tmp[s], gb[:, 0:D], ALU.mult).then_inc(ln_step, ONE)
                    for s in range(2):
                        dve.wait_ge(ln_step, 4 * (4 * n) + 4 * i + 2 + s + 1)
                        nc.vector.tensor_tensor(tmp[s], tmp[s], gb[:, D:2 * D], ALU.add).then_inc(xn_done, ONE)
                    if turn:
                        for s in range(2):
                            turn_in(n + 1, i, s)

            def ffn(l, B):
                def other_taps(i, q):
                    dve.wait_ge(tap0_done, B.tap + 4 * i + q + 1)
                    b = q % 2
                    nc.vector.scalar_tensor_tensor(out=tmp[q][:, 1:T], in0=up[b][:, 0:T - 1], scalar=tap(l, 1, q, i),
                                                   in1=tmp[q][:, 1:T], op0=ALU.mult, op1=ALU.add).then_inc(tap1_done, ONE)
                    dve.wait_ge(tap1_done, B.tap + 4 * i + q + 1)
                    nc.vector.scalar_tensor_tensor(out=tmp[q][:, 2:T], in0=up[b][:, 0:T - 2], scalar=tap(l, 0, q, i),
                                                   in1=tmp[q][:, 2:T], op0=ALU.mult, op1=ALU.add).then_inc(up_free[b], ONE)

                def chunk(i, split_next):
                    for q in range(4):
                        if q < 2 or split_next:
                            lo_col(B, 2 * i + 1 + q // 2, q % 2)
                        other_taps(i, q)
                        if q >= 2:
                            s = q - 2
                            dve.wait_ge(up_free[s], freed(B.up, 1) + 2 * i)
                            dve.wait_ge(gate_act, B.tap // 2 + 2 * i + s + 1)
                            nc.vector.tensor_tensor(tmp[q], tmp[q], tmp[s], ALU.mult).then_inc(y_done, ONE)
                            hid_lo_part(B, i, s)
                        if q == 1:
                            for k in range(2):
                                lo_wide(B.wide + 2 * i + k, k)
                    add_down(B.down + TT * i)

                with dve.Fori(0, FI - 1) as i:
                    chunk(i, True)
                with dve.Fori(FI - 1, FI) as i:
                    chunk(i, l == 0)

            layer_norm(0, True)
            ffn(0, F1)
            layer_norm(1, True)
            for k in range(2):
                lo_wide(V2.wide + k, k)
            for s in range(2):
                lo_col(AT, 0, s)
            dve.wait_ge(attn_v_stored, 4 * DMA)
            with dve.Fori(0, NPAIR) as i:
                m = AT.up + PAIR_UP * i
                m2 = PAIR_UP // 2 * i
                lo_col(AT, 2 * i + 1, 0)
                lo_col(AT, 2 * i + 1, 1)
                lo_wide(AT.wide + i, 0)
                lo_col(AT, 2 * i + 2, 0)
                for g in (2, 1, 0):
                    if g == 1:
                        lo_col(AT, 2 * i + 2, 1)
                    st = steps(g)
                    dve.wait_ge(bias_in[g], (4 if g == 2 else 2) * DMA * (i + 1))
                    for k in range(8 + 1):
                        if k < 8:
                            t, keys, w = st[k]
                            b = (STEP_UP[g] + k) % 2
                            wait_apart(dve, (up_done, m + STEP_UP[g] + k + 1))
                            for h in range(2):
                                nc.vector.tensor_tensor_reduce(prob[k % 2][:, h, 0:w], up[b][:, h * HALF:h * HALF + w],
                                                               bias[g][:, h, b_w[g] - w:b_w[g]], 1.0, 3e38, ALU.add, ALU.min,
                                                               nat[g][:, k, 2 * HD + h:2 * HD + h + 1]
                                                               ).then_inc(up_free[b] if h else logits_a, ONE)
                        if k >= 1:
                            j = k - 1
                            w = st[j][2]
                            dve.wait_ge(turned, 24 * i + STEP_DOWN[g] + j + 1)
                            dve.wait_ge(down_done, AT.down + PAIR_DOWN * i + STEP_DOWN[g] + j - 1)
                            nc.vector.tensor_copy(prob_t[j % 2][:, :, 0:w],
                                                  down[j % 2][:, 0:HALF].rearrange("p (h w) -> p h w", h=2)[:, :, 0:w]
                                                  ).then_inc(prob_t_ready, ONE)
                MIX = 11
                count = [0]

                def link(ins):
                    ins.then_inc(mix_step, ONE)
                    count[0] += 1
                    dve.wait_ge(mix_step, MIX * i + count[0])

                for g in (1, 2):
                    dve.wait_ge(nat_in[g], DMA * i + DMA)
                for b in range(2):
                    dve.wait_ge(down_free[b], freed(AT.down + STEP_DOWN[0], 3) + PAIR_DOWN // 2 * i)

                def stat(g, at):
                    return nat[g][:, :, 2 * HD + at:2 * HD + at + 2]

                def small(n):
                    return mix[:, 16 * n:16 * n + 16].rearrange("p (t h) -> p t h", t=TT)

                tt = nc.vector.tensor_tensor
                link(tt(small(0), stat(0, 0), stat(1, 0), ALU.min))
                link(tt(small(0), small(0), stat(2, 0), ALU.min))
                for g in range(3):
                    last = tt(small(1 + g), small(0), stat(g, 0), ALU.subtract)
                last.then_inc(mix_delta, ONE)
                dve.wait_ge(mix_exp, i + 1)
                for g in range(3):
                    last = tt(small(4 + g), small(1 + g), stat(g, 2), ALU.mult)
                link(last)
                link(tt(small(4), small(4), small(5), ALU.add))
                link(tt(small(4), small(4), small(6), ALU.add))
                link(nc.vector.reciprocal(small(7), small(4)))
                for g in range(3):
                    last = tt(small(1 + g), small(1 + g), small(7), ALU.mult)
                link(last)
                for g in range(3):
                    v = nat[g][:, :, 0:2 * HD].rearrange("p t (h d) -> p t h d", h=2)
                    wb = small(1 + g).rearrange("p t (h o) -> p t h o", o=1).to_broadcast([P, TT, 2, HD])
                    link(tt(v, v, wb, ALU.mult))
                o = q_t[0].rearrange("p (t c) -> p t c", t=TT)
                link(tt(o, nat[0][:, :, 0:2 * HD], nat[1][:, :, 0:2 * HD], ALU.add))
                tt(o, o, nat[2][:, :, 0:2 * HD], ALU.add).then_inc(o_done, ONE)
                for b in range(2):
                    dve.wait_ge(o_hi_done, 2 * i + b + 1)
                    tt(hid_lo[:, 0, b * HALF:(b + 1) * HALF], up[b][:, 0:HALF], hid_hi[:, 0, b * HALF:(b + 1) * HALF],
                       ALU.subtract).then_inc(up_free[b], ONE)
                add_down(AT.down + PAIR_DOWN * i + 24)
            layer_norm(2, True)
            ffn(1, F2)
            layer_norm(3, False)

        @block.tensor
        def _(pe):
            for b in range(2):
                pe.sem_inc(up_free[b], 1)
                pe.sem_inc(down_free[b], DOWN0 // 2 + 1)
            pe.sem_inc(down_done, DOWN0)

            def mm(o, a, b, start, stop, **kw):
                return nc.tensor.matmul(o, a, b, start=start, stop=stop, **kw)

            def split_mm(o, a, b, first, last):
                mm(o, a[0], b[0], first, False)
                mm(o, a[0], b[1], False, False)
                return mm(o, a[1], b[0], False, last)

            def up_free_for(at, j):
                pe.wait_ge(up_free[at % 2], at // 2 + 1 + j)

            def turn_x(at, i, s):
                up_free_for(at + s, i)
                for k in range(KT):
                    last = nc.tensor.transpose(up[s][:, k * P:(k + 1) * P], tmp[s][:, k * P:(k + 1) * P], ident[:])
                last.then_inc(up_done, ONE)

            def features(at, j, piece, s):
                pe.wait_ge(col_lo_done, piece + 3)
                up_free_for(at, j)
                for h in range(2):
                    for k in range(KT):
                        sl = slice(h * HALF, (h + 1) * HALF)
                        last = split_mm(up[at % 2][:, sl], (col_hi[:, s, k], col_lo[:, s, k]),
                                        (xt_hi[:, k, sl], xt_lo[:, k, sl]), k == 0, k == KT - 1)
                last.then_inc(up_done, ONE)

            def down_unit(at, j, nk):
                for t in range(TT):
                    b = t % 2
                    pe.wait_ge(down_free[b], at // 2 + t // 2 + 1 + j)
                    for n in range(2):
                        sl = slice(n * HALF, (n + 1) * HALF)
                        tk = slice(t * P, (t + 1) * P)
                        for k in range(nk):
                            last = split_mm(down[b][:, sl], (hid_hi[:, k, tk], hid_lo[:, k, tk]),
                                            (wide_hi[:, k, sl], wide_lo[:, k, sl]), k == 0, k == nk - 1)
                    last.then_inc(down_done, ONE)

            def v_unit(at, j, hi, lo):
                for q in range(2):
                    up_free_for(at + q, j)
                    for t in range(4):
                        tk = slice((4 * q + t) * P, (4 * q + t + 1) * P)
                        o = up[q][:, t * 2 * P:(t + 1) * 2 * P].rearrange("p (s n) -> p s n", s=2)
                        for k in range(KT):
                            last = split_mm(o, (xt_hi[:, k, tk], xt_lo[:, k, tk]), (hi[:, :, k], lo[:, :, k]),
                                            k == 0, k == KT - 1)
                    last.then_inc(up_done, ONE)

            pe.wait_ge(ident_in, DMA)
            with pe.Fori(0, TT // 2) as i:
                for s in range(2):
                    pe.wait_ge(x_in[s], DMA * i + DMA)
                    turn_x(X_UP, i, s)
            pe.wait_ge(par_in, 10 * DMA)
            up_free_for(SET_UP, 0)
            for blk in range(4):
                last = nc.tensor.transpose(up[0][:, blk * P:blk * P + 88], tmp[2][0:88, blk * P:(blk + 1) * P], ident[0:88, 0:88])
            last.then_inc(up_done, ONE)
            up_free_for(SET_UP + 1, 0)
            nc.tensor.transpose(up[1][:, 0:32], tmp[2][0:32, 4 * P:5 * P], ident[0:32, 0:32]).then_inc(up_done, ONE)
            pe.wait_ge(tab_in, 2 * DMA)
            pe.wait_ge(consts_ready, 2)
            up_free_for(SET_UP + 2, 0)
            for g in range(2):
                last = mm(up[0][0:8, g * HALF:g * HALF + TABW], table[0:33, 8 * g:8 * g + 8],
                          pick[0:33, g * TABW:(g + 1) * TABW], True, True)
            last.then_inc(up_done, ONE)
            up_free_for(SET_UP + 3, 0)
            mm(up[1][0:8, 0:TABW], table[0:33, 16:24], pick[0:33, 2 * TABW:3 * TABW], True, True).then_inc(up_done, ONE)
            pe.wait_ge(ws_masked, 1)
            up_free_for(SET_UP + 4, 0)
            for g in range(SG):
                last = nc.tensor.transpose(up[0][:, g * P:(g + 1) * P], ws_t[:, g * P:(g + 1) * P], ident[:])
            last.then_inc(up_done, ONE)
            pe.wait_ge(up_free[0], freed(SET_UP, 2))
            up_free_for(SET_UP + 5, 0)
            for h in range(2):
                last = mm(up[1][:, h * HALF:(h + 1) * HALF], ones, ws_t[:, h * HALF:(h + 1) * HALF], True, True)
            last.then_inc(up_done, ONE)

            wait_turned(pe, 0)
            with pe.Fori(0, 4) as i:
                pe.wait_ge(col_lo_done, V1.col + 2 * i + 4)
                v_unit(V1.up, 2 * i, col_hi, col_lo)
                pe.wait_ge(wide_lo_done, V1.wide + 2 * i + 4)
                v_unit(V1.up + 2, 2 * i, wide_k_hi, wide_k_lo)

            def mixed(i, s):
                pe.wait_ge(v_norm, 2 * i + s + 1)
                up_free_for(G1.up + 2 * s + 1, 2 * i)
                for t in range(TT):
                    last = mm(up[1][:, t * P:(t + 1) * P], v_in[s][:, t * P:(t + 1) * P],
                              ws_t.rearrange("p (g t) -> p g t", g=SG)[:, ds(i, 1)].rearrange("p a t -> p (a t)"), True, True)
                last.then_inc(up_done, ONE)

            def gated(i, last_group):
                mixed(i, 0)
                features(G1.up + 2, 2 * i, G1.col + 2 * i + 1, 1)
                mixed(i, 1)
                if not last_group:
                    features(G1.up + 4, 2 * i, G1.col + 2 * i + 2, 0)
                pe.wait_ge(hid_ready, G1.hid + 2 * i + 2)
                pe.wait_ge(wide_lo_done, G1.wide + 2 * i + 4)
                down_unit(G1.down, 4 * i, 2)

            features(G1.up, 0, G1.col, 0)
            with pe.Fori(0, SG - 1) as i:
                gated(i, False)
            with pe.Fori(SG - 1, SG) as i:
                gated(i, True)

            def layer_norm(n):
                with pe.Fori(0, TT // 2) as i:
                    for s in range(2):
                        pe.wait_ge(xn_done, TT * n + 2 * i + s + 1)
                        turn_x(LN_UP[n], i, s)
                wait_turned(pe, n + 1)

            def ffn(B):
                def chunk(i, last_chunk):
                    for q in range(1, 4):
                        features(B.up + q, 2 * i, B.col + 4 * i + q, q % 2)
                    if not last_chunk:
                        features(B.up + 4, 2 * i, B.col + 4 * i + 4, 0)
                    pe.wait_ge(hid_ready, B.hid + 2 * i + 2)
                    pe.wait_ge(wide_lo_done, B.wide + 2 * i + 4)
                    down_unit(B.down, 4 * i, 2)

                features(B.up, 0, B.col, 0)
                with pe.Fori(0, FI - 1) as i:
                    chunk(i, False)
                with pe.Fori(FI - 1, FI) as i:
                    chunk(i, True)

            layer_norm(0)
            ffn(F1)
            layer_norm(1)
            pe.wait_ge(col_lo_done, V2.col + 4)
            v_unit(V2.up, 0, col_hi, col_lo)
            pe.wait_ge(wide_lo_done, V2.wide + 4)
            v_unit(V2.up + 2, 0, wide_k_hi, wide_k_lo)
            with pe.Fori(0, NPAIR) as i:
                m2 = PAIR_UP // 2 * i
                d2 = PAIR_DOWN // 2 * i
                for f in range(3):
                    features(AT.up + f, m2, AT.col + 4 * i + f, f % 2)
                pe.wait_ge(up_free[0], freed(AT.up, 0) + m2)
                for g in (2, 1, 0):
                    if g == 1:
                        features(AT.up + Q0_UP, m2, AT.col + 4 * i + 3, 1)
                    f = {2: 1, 1: 2, 0: Q0_UP}[g]
                    pe.wait_ge(up_free[f % 2], freed(AT.up + f - f % 2, 0) + m2)
                    q = q_t[1 if g == 1 else 0]
                    v = v_perm[1 if g == 1 else 0]
                    st = steps(g)
                    for k in range(8 + 2):
                        if k < 8:
                            t, keys, w = st[k]
                            f = STEP_UP[g] + k
                            up_free_for(AT.up + f, m2)
                            for h in range(2):
                                hp = slice(h * HD, (h + 1) * HD)
                                queries = q[hp, t * P:(t + 1) * P] if g == 2 else tokens(q[hp], g, t, 1)
                                last = mm(up[f % 2][:, h * HALF:h * HALF + w], queries,
                                          tokens(k_t[hp], g, t, len(keys)), True, True)
                            last.then_inc(up_done, ONE)
                        if 1 <= k <= 8:
                            j = k - 1
                            pe.wait_ge(exp_done, 24 * i + STEP_DOWN[g] + j + 1)
                            pe.wait_ge(down_free[j % 2], (AT.down + STEP_DOWN[g] + j) // 2 + 1 + d2)
                            for h in range(2):
                                for c in range(len(st[j][1])):
                                    last = nc.tensor.transpose(down[j % 2][:, h * 2 * P + c * P:h * 2 * P + (c + 1) * P],
                                                               prob[j % 2][:, h, c * P:(c + 1) * P], ident[:])
                            last.then_inc(turned, ONE)
                        if k >= 2:
                            j = k - 2
                            if j == 0:
                                pe.wait_ge(vp_in[g], {2: 2, 1: 4, 0: 1}[g] * DMA * (i + 1))
                            pe.wait_ge(prob_t_ready, 24 * i + STEP_DOWN[g] + j + 1)
                            keys = st[j][1]
                            for h in range(2):
                                for c, t in enumerate(keys):
                                    last = mm(down[j % 2][:, HALF + h * HD:HALF + (h + 1) * HD],
                                              prob_t[j % 2][:, h, c * P:(c + 1) * P], v[:, t, h * HD:(h + 1) * HD],
                                              c == 0, c == len(keys) - 1)
                            last.then_inc(down_done, ONE)
                pe.wait_ge(o_done, i + 1)
                for b in range(2):
                    up_free_for(AT.up + TURN_UP + b, m2)
                    for t in range(4):
                        c = (4 * b + t) * P
                        last = nc.tensor.transpose(up[b][:, t * P:(t + 1) * P], q_t[0][:, c:c + P], ident[:])
                    last.then_inc(up_done, ONE)
                for b in range(2):
                    pe.wait_ge(up_free[b], freed(AT.up + TURN_UP, 0) + m2)
                pe.wait_ge(wide_lo_done, AT.wide + i + 3)
                down_unit(AT.down + 24, PAIR_DOWN // 2 * i, 1)
            layer_norm(2)
            ffn(F2)


_INS = ['x', 'a_w_in', 'a_ln_g', 'a_ln_b', 'a_w_s', 'a_b_s', 'a_w_out', 'kv_w', 'b_w_q', 'b_w_o', 'rel_table',
        'ffn_w_up', 'ffn_conv_w', 'ffn_conv_b', 'ffn_w_down', 'ln_g', 'ln_b']
_OUT = (1, T, D)


def bucket_pick_constant():
    import numpy as np
    pick = np.zeros((33, len(DIL), TABW), np.float32)
    for g, dil in enumerate(DIL):
        for j in range(TABW):
            delta = 255 - j
            if not 0 <= delta <= 128:
                pick[32, g, j] = 1.0
                continue
            n = delta * dil
            bucket = n
            if n >= 16:
                scaled = np.log(np.float32(n) / np.float32(16)) / np.float32(np.log(2048 / 16)) * np.float32(16)
                bucket = min(16 + int(np.float32(scaled)), 31)
            pick[bucket, g, j] = -1.0
    return pick.reshape(33, len(DIL) * TABW)


def kernel(**inputs):
    import numpy as _np
    import concourse.bacc as _bacc
    from concourse import mybir as _mybir
    from concourse.bass_utils import run_bass_kernel_spmd as _run

    nc = _bacc.Bacc("TRN2", target_bir_lowering=False, num_devices=1)
    arrays, args = {}, []

    def give(name, a):
        arrays[f"in_{name}_dram"] = a
        args.append(nc.dram_tensor(f"in_{name}_dram", a.shape, _mybir.dt.from_np(a.dtype), kind="ExternalInput").ap())

    for name in _INS:
        give(name, _np.ascontiguousarray(inputs[name]))
    give("bucket_pick", bucket_pick_constant())
    give("identity", _np.eye(P, dtype=_np.float32))
    args.append(nc.dram_tensor("out_0_dram", _OUT, _mybir.dt.float32, kind="ExternalOutput").ap())
    program(nc, *args)
    r = _run(nc, [arrays], core_ids=[0])
    return r.results[0]["out_0_dram"]
```

```python
from contextlib import ExitStack

import concourse.bass as bass
from concourse import mybir

F32 = mybir.dt.float32
F32R = mybir.dt.float32r
ACT = mybir.ActivationFunctionType
ALU = mybir.AluOpType
ds = bass.ds

P = 128
T = 1024
D = 1024
KT = D // P
TT = T // P
HALF = 512
W_SGU = 2048
CT = W_SGU // P
SG = 8
D_FF = 2816
FT = D_FF // P
FI = FT // 2
HD = 64
NPAIR = 4
DIL = (1, 4, 16)
TABW = 384
ROW = 2 * HD + 4
ALPHA = 4 ** 0.25
EPS = 1e-5
BIG = 1e30
ONE = 1
DMA = 16


def program(nc, x, a_w_in, a_ln_g, a_ln_b, a_w_s, a_b_s, a_w_out, kv_w, b_w_q, b_w_o, rel_table,
            ffn_w_up, ffn_conv_w, ffn_conv_b, ffn_w_down, ln_g, ln_b, bucket_pick, identity, out):
    ctx = ExitStack()
    with ctx:
        def sb(name, shape, dt=F32):
            return ctx.enter_context(nc.sbuf_tensor(name, shape, dt))

        def sem(name):
            return ctx.enter_context(nc.semaphore(name))

        xt_hi = sb("xt_hi", [P, KT, T], F32R)
        xt_lo = sb("xt_lo", [P, KT, T], F32R)
        col_hi = sb("col_hi", [P, 2, KT, P], F32R)
        col_lo = sb("col_lo", [P, 2, KT, P], F32R)
        wide_hi = sb("wide_hi", [P, 2, D], F32R)
        wide_lo = sb("wide_lo", [P, 2, D], F32R)
        hid_hi = sb("hid_hi", [P, 2, T], F32R)
        hid_lo = sb("hid_lo", [P, 2, T], F32R)
        res = sb("res", [P, TT, D])
        raw_col = sb("raw_col", [P, 2, KT, P])
        raw_wide = sb("raw_wide", [P, 2, D])
        par = sb("par", [P, 5, 88])
        ident = sb("ident", [P, P])
        WORK = 11616
        work = sb("work", [P, WORK])

        def view(at, n):
            return work[:, at:at + n]

        tmp = [view(K * T, T) for K in range(4)]
        bias_ts = view(4096, 2048).rearrange("p (c t) -> p c t", c=CT)
        ws_t = view(6144, 1024)
        v_in = [view(7168 + s * 1024, 1024) for s in range(2)]
        bs_rows = view(7168, 1024)
        ones = view(8192, P)
        v_stats = view(9216, TT * 8 * 6).rearrange("p (t j x) -> p t j x", t=TT, j=8)
        gb = view(9216, 2 * D)
        v_mv = view(11264, 2 * TT).rearrange("p (t x) -> p t x", x=2)
        ln_mv = view(11280, 2 * TT).rearrange("p (t x) -> p t x", x=2)
        v_rstd = view(11296, TT)
        ln_rstd = view(11304, TT)
        v_half = view(11312, TT)
        ln_stats = view(11320, TT * 12).rearrange("p (t j x) -> p t j x", t=TT, j=2)
        nat = [view(g * TT * ROW, TT * ROW).rearrange("p (t r) -> p t r", t=TT) for g in range(3)]
        k_t = view(3168, T)
        q_t = [view(4192 + s * T, T) for s in range(2)]
        v_perm = [view(6240 + s * T, T).rearrange("p (t c) -> p t c", t=TT) for s in range(2)]
        b_at = [8288, 8800, 9312]
        b_w = [256, 256, 128]
        bias = [view(b_at[g], 2 * b_w[g]).rearrange("p (h w) -> p h w", h=2) for g in range(3)]
        prob = [a.rearrange("p (h w) -> p h w", h=2)
                for a in (view(9568, 512), view(10080, 512), raw_wide[:, 1, 0:512], raw_wide[:, 1, 512:1024])]
        prob_t = [view(10592 + s * 512, 512).rearrange("p (h w) -> p h w", h=2) for s in range(2)]
        mix = view(9568, 160)
        table = view(9600, 24)
        pick = view(9632, 3 * TABW)
        tab_rows = view(4096, 3 * TABW)

        up = [ctx.enter_context(nc.psum_tensor(f"up{b}", [P, 2 * HALF], F32)) for b in range(2)]
        down = [ctx.enter_context(nc.psum_tensor(f"down{b}", [P, 2 * HALF], F32)) for b in range(2)]

        v_dram = nc.dram_tensor("v_scratch", [CT, P, TT * P], F32).ap()
        vnat_dram = nc.dram_tensor("attn_v_scratch", [T, 4 * P], F32).ap()
        o_dram = nc.dram_tensor("attn_out_scratch", [2, T, ROW], F32).ap()
        tab_dram = nc.dram_tensor("bias_rows_scratch", [24, TABW], F32).ap()
        skew_dram = nc.dram_tensor("bias_skew_scratch", [24, P * TABW], F32).ap()

        ident_in, par_in = sem("ident_in"), sem("par_in")
        ws_in, bs_in, tab_in = sem("ws_in"), sem("bs_in"), sem("tab_in")
        x_in = [sem(f"x_in{t}") for t in range(TT)]
        pool_step = sem("pool_step")
        consts_ready = sem("consts_ready")
        tab_stored, skew_stored = sem("tab_stored"), sem("skew_stored")
        ws_masked = sem("ws_masked")
        col_in = [sem(f"col_in{s}") for s in range(2)]
        wide_in = [sem(f"wide_in{s}") for s in range(2)]
        col_hi_done, col_lo_done = sem("col_hi_done"), sem("col_lo_done")
        wide_hi_done, wide_lo_done = sem("wide_hi_done"), sem("wide_lo_done")
        up_done, down_done = sem("up_done"), sem("down_done")
        up_free = [sem(f"up_free{b}") for b in range(2)]
        down_free = [sem(f"down_free{b}") for b in range(2)]
        xt_hi_done, res_scaled = sem("xt_hi_done"), sem("res_scaled")
        v_counted = sem("v_counted")
        v_stored = [sem(f"v_stored{k}") for k in range(4)]
        v_mean, v_scale, v_norm = sem("v_mean"), sem("v_scale"), sem("v_norm")
        v_loaded = [sem(f"v_loaded{s}") for s in range(2)]
        tap0_done, tap1_done, gate_act = sem("tap0_done"), sem("tap1_done"), sem("gate_act")
        y_done, hid_hi_done, hid_ready = sem("y_done"), sem("hid_hi_done"), sem("hid_ready")
        gb_in = sem("gb_in")
        ln_counted, ln_mean, ln_scale = sem("ln_counted"), sem("ln_mean"), sem("ln_scale")
        ln_step, xn_done = sem("ln_step"), sem("xn_done")
        out_stored = [sem(f"out_stored{s}") for s in range(4)]
        attn_v_stored = sem("attn_v_stored")
        logits_a, exp_done, turned, prob_t_ready = sem("logits_a"), sem("exp_done"), sem("turned"), sem("prob_t_ready")
        vp_in = [sem(f"vp_in{g}") for g in range(3)]
        bias_in = [sem(f"bias_in{g}") for g in range(3)]
        bias_clear = sem("bias_clear")
        nat_stored = [None, sem("nat_stored1"), sem("nat_stored2")]
        nat_in = [None, sem("nat_in1"), sem("nat_in2")]
        mix_step, mix_delta, mix_exp = sem("mix_step"), sem("mix_delta"), sem("mix_exp")
        o_done, o_hi_done = sem("o_done"), sem("o_hi_done")

        class Base:
            def __init__(self, col, wide, in0, up, in1=0, down=0, hid=0, tap=0):
                self.col, self.wide, self.in0, self.in1 = col, wide, in0, in1
                self.up, self.down, self.hid, self.tap = up, down, hid, tap

        SET_UP = 0
        X_DOWN = TT
        V1 = Base(col=0, wide=0, in0=0, in1=0, up=SET_UP + 6)
        G1 = Base(col=8, wide=8, in0=4, in1=4, up=V1.up + 16, down=X_DOWN + TT, hid=0)
        LN_DOWN = [G1.down + TT * SG]
        F1 = Base(col=G1.col + 2 * SG, wide=G1.wide + 2 * SG, in0=G1.in0 + SG, in1=G1.in1 + SG, up=G1.up + 4 * SG,
                  down=LN_DOWN[0] + TT, hid=2 * SG, tap=0)
        LN_DOWN.append(F1.down + TT * FI)
        V2 = Base(col=F1.col + 4 * FI, wide=F1.wide + 2 * FI, in0=F1.in0 + FI, in1=F1.in1 + FI, up=F1.up + 4 * FI,
                  down=LN_DOWN[1] + TT)
        PAIR_UP, PAIR_DOWN = 30, 24 + TT
        AT = Base(col=V2.col + 2, wide=V2.wide + 2, in0=V2.in0 + 1, up=V2.up + 4, down=V2.down)
        LN_DOWN.append(AT.down + NPAIR * PAIR_DOWN)
        F2 = Base(col=AT.col + 4 * NPAIR, wide=AT.wide + NPAIR, in0=AT.in0 + NPAIR, in1=V2.in1 + 1,
                  up=AT.up + NPAIR * PAIR_UP, down=LN_DOWN[2] + TT, hid=F1.hid + 2 * FI, tap=4 * FI)
        LN_DOWN.append(F2.down + TT * FI)
        Q2_UP, Q0_UP, NEXT_UP = 2, 11, 28
        ORDER = (2, 1, 0)
        STEP_DOWN = {2: 0, 1: 8, 0: 16}

        def step_up(k):
            return 3 + k if k < 8 else 4 + k

        def freed(base, j, more=0):
            return base // 2 + j + 2 + more

        def wait_apart(eng, *waits):
            waits = [(to, eng.to_reg(value)) for to, value in waits]
            eng.wait_ge(consts_ready, 2)
            for to, value in waits:
                eng.wait_ge(to, value)

        def wait_turned(eng, n, tiles=TT):
            at = X_DOWN if n == 0 else LN_DOWN[n - 1]
            for b in range(2):
                eng.wait_ge(down_free[b], freed(at, (tiles - 1 - b) // 2))

        def col_piece(w, at, i, step):
            n = w.shape[1] // (step * P)
            v = w.rearrange("(k p) (i s n) -> i s p k n", p=P, s=step, n=P)
            return v[ds(i, 1), at].rearrange("a p k n -> (a p) k n")

        def row_piece(w, at, i, step):
            v = w.rearrange("(i s p) n -> i s p n", s=step, p=P)
            return v[ds(i, 1), at].rearrange("a p n -> (a p) n")

        w_u, w_v = a_w_in[0][:, 0:W_SGU], a_w_in[0][:, W_SGU:2 * W_SGU]
        w_out, w_q, w_o = a_w_out[0], b_w_q[0], b_w_o[0]
        w_k, w_kv = kv_w[:, 0:4 * P], kv_w[:, 4 * P:8 * P]
        xt_hi_t = xt_hi[:].rearrange("p k (i s t) -> p k i s t", s=2, t=P)
        xt_lo_t = xt_lo[:].rearrange("p k (i s t) -> p k i s t", s=2, t=P)
        res_t = res[:].rearrange("p (i s) d -> p i s d", s=2)
        wide_k_hi = wide_hi[:].rearrange("p s (k n) -> p s k n", n=P)
        wide_k_lo = wide_lo[:].rearrange("p s (k n) -> p s k n", n=P)
        conv = par[:, 0:4, :].rearrange("p (l b) (j g i s) -> p l b j g i s", l=2, j=2, g=2, s=2)

        def tap(l, k, q, i):
            return conv[:, l, k // 2, k % 2, q // 2, ds(i, 1), q % 2]

        def tok_tile(a, i, s):
            return a[:, :, ds(i, 1), s].rearrange("p k a t -> p k (a t)")

        def res_tile(i, s):
            return res_t[:, ds(i, 1), s].rearrange("p a d -> p (a d)")

        def steps():
            out = []
            for g in ORDER:
                for k in range(8):
                    first = (k == 0, k % 2 == 0, True)[g]
                    out.append((g, k, [k] if first else [k - 1, k], P if first else 2 * P))
            return out

        def tokens(a, g, t, n):
            if g == 0:
                return a[:, (t + 1 - n) * P:(t + 1) * P]
            if g == 1:
                v = a.rearrange("p (s r) -> p r s", r=4)[:, t // 2]
                return v if n == 2 else v[:, (t % 2) * P:(t % 2 + 1) * P]
            return a.rearrange("p (s t h) -> p t h s", t=8, h=2)[:, t]

        block = ctx.enter_context(nc.Block())

        @block.sync
        def _(sp):
            def col_load(B, j, s, src):
                sp.wait_ge(col_lo_done, B.col + 2 * j + s + 1)
                sp.dma_start(raw_col[:, s], src).then_inc(col_in[s], DMA)

            def wide_load(B, j, s, src):
                sp.wait_ge(wide_lo_done, B.wide + 2 * j + s + 1)
                sp.dma_start(raw_wide[:, s], src).then_inc(wide_in[s], DMA)

            def wide_col_load(B, j, s, src):
                sp.wait_ge(wide_lo_done, B.wide + 2 * j + s + 1)
                sp.dma_start(raw_wide[:, s].rearrange("p (k n) -> p k n", n=P), src).then_inc(wide_in[s], DMA)

            sp.dma_start(ident[:], identity).then_inc(ident_in, DMA)
            for t in range(TT):
                sp.dma_start(res[:, t], x[0, t * P:(t + 1) * P]).then_inc(x_in[t], DMA)

            def v_loads(i):
                for k in range(2):
                    col_load(V1, i, k, col_piece(w_v, k, i, 4))
                for k in range(2):
                    wide_col_load(V1, i, k, col_piece(w_v, 2 + k, i, 4))

            with sp.Fori(0, 1) as i:
                v_loads(i)
            rows = tmp[2]
            for l in range(2):
                for k in range(4):
                    src = ffn_conv_w[l, k:k + 1] if k < 3 else ffn_conv_b[l:l + 1]
                    sp.dma_start(rows[44 * (k % 2):44 * (k % 2) + 44, (2 * l + k // 2) * P:(2 * l + k // 2 + 1) * P],
                                 src.rearrange("a (r n) -> (a r) n", n=P)).then_inc(par_in, DMA)
            for k, src in enumerate((a_ln_g, a_ln_b)):
                sp.dma_start(rows[CT * k:CT * (k + 1), 4 * P:5 * P],
                             src.rearrange("a (r n) -> (a r) n", n=P)).then_inc(par_in, DMA)
            sp.wait_ge(consts_ready, 1)
            sp.dma_start(table[0:32, :], rel_table).then_inc(tab_in, DMA)
            sp.dma_start(pick[0:33, :], bucket_pick).then_inc(tab_in, DMA)
            sp.dma_start(ws_t.rearrange("p (g s) -> p g s", g=SG), a_w_s[0].rearrange("g t s -> t g s")).then_inc(ws_in, DMA)
            sp.dma_start(bs_rows, a_b_s.rearrange("a g t -> a (g t)").to_broadcast([P, SG * P])).then_inc(bs_in, DMA)
            with sp.Fori(1, 4) as i:
                v_loads(i)
            with sp.Fori(0, SG) as i:
                for s in range(2):
                    col_load(G1, i, s, col_piece(w_u, s, i, 2))
                for k in range(2):
                    wide_load(G1, i, k, row_piece(w_out, k, i, 2))

            def ffn_loads(l, B):
                wu, wd = ffn_w_up[l], ffn_w_down[l]
                with sp.Fori(0, FI) as i:
                    for q in range(4):
                        half = wu[:, (q // 2) * D_FF:(q // 2 + 1) * D_FF]
                        col_load(B, 2 * i + q // 2, q % 2, col_piece(half, q % 2, i, 2))
                        if q % 2:
                            if l and q == 1:
                                sp.wait_ge(wide_lo_done, B.wide + 2)
                            if l and q == 3:
                                sp.wait_ge(o_done, NPAIR)
                            wide_load(B, i, q // 2, row_piece(wd, q // 2, i, 2))

            ffn_loads(0, F1)
            with sp.Fori(0, 1) as i:
                for k in range(2):
                    col_load(V2, i, k, col_piece(w_kv, k, i, 4))
                for k in range(2):
                    wide_col_load(V2, i, k, col_piece(w_kv, 2 + k, i, 4))
            with sp.Fori(0, NPAIR) as i:
                for q, src in enumerate((w_k, w_q[:, 4 * P:8 * P], w_q[:, 8 * P:12 * P], w_q[:, 0:4 * P])):
                    col_load(AT, 2 * i + q // 2, q % 2, col_piece(src, 0, i, 1))
                sp.wait_ge(wide_lo_done, AT.wide + i + 2)
                sp.dma_start(raw_wide[:, 0], row_piece(w_o, 0, i, 1)).then_inc(wide_in[0], DMA)
            ffn_loads(1, F2)
            for t in range(TT):
                sp.wait_ge(xn_done, 3 * TT + t + 1)
                sp.dma_start(out[0, t * P:(t + 1) * P], tmp[t % 4]).then_inc(out_stored[t % 4], DMA)
            for s in range(4):
                sp.wait_ge(out_stored[s], DMA * TT // 4)

        @block.gpsimd
        def _(pool):
            nc.gpsimd.memset(table[0:33, :], BIG).then_inc(consts_ready, ONE)
            nc.gpsimd.memset(ones, 1.0).then_inc(consts_ready, ONE)
            nc.gpsimd.memset(v_half, -0.5).then_inc(pool_step, ONE)
            pool.wait_ge(ws_in, DMA)
            wv = ws_t.rearrange("p (g s) -> p g s", g=SG)
            nc.gpsimd.affine_select(out=wv, in_=wv, compare_op=ALU.is_ge, fill=0.0, base=0,
                                    pattern=[[0, SG], [-1, P]], channel_multiplier=1).then_inc(ws_masked, ONE)
            for b in range(2):
                pool.wait_ge(up_free[b], freed(SET_UP, 1))
            for g in range(3):
                pool.dma_start(tab_dram[8 * g:8 * g + 8], tab_rows[0:8, g * TABW:(g + 1) * TABW]).then_inc(tab_stored, DMA)
            pool.wait_ge(tab_stored, 3 * DMA)
            for g in range(3):
                src = bass.AP(tensor=tab_dram.tensor, offset=8 * g * TABW, ap=[[TABW, 8], [0, P], [1, TABW]])
                pool.dma_start(skew_dram[8 * g:8 * g + 8].rearrange("h (p w) -> h p w", w=TABW), src).then_inc(skew_stored, DMA)
            vd = v_dram.rearrange("(i u c) p (q t n) -> i u c q p t n", u=2, c=2, q=2, t=4)
            with pool.Fori(0, 4) as i:
                for k in range(4):
                    u, q = k // 2, k % 2
                    wait_apart(pool, (up_free[q], freed(V1.up, u) + 2 * i))
                    for c in range(2):
                        pool.dma_start(vd[ds(i, 1), u, c, q].rearrange("a p t n -> (a p) t n"),
                                       tmp[k].rearrange("p (t c n) -> p t c n", t=4, c=2)[:, :, c, :]
                                       ).then_inc(v_stored[k], DMA)
            pool.wait_ge(v_mean, TT)
            nc.gpsimd.tensor_scalar(v_rstd, v_mv[:, :, 1], EPS, None, ALU.add).then_inc(pool_step, ONE)
            pool.wait_ge(pool_step, 2)
            nc.gpsimd.tensor_tensor(v_rstd, v_rstd, v_half, ALU.pow).then_inc(v_scale, ONE)
            for k in range(4):
                pool.wait_ge(v_stored[k], 8 * DMA)
            vl = v_dram.rearrange("(i s) p n -> i s p n", s=2)
            pool.wait_ge(up_free[1], freed(SET_UP, 2))
            with pool.Fori(0, SG) as i:
                for s in range(2):
                    wait_apart(pool, (up_done, G1.up + 4 * i - 2 + 2 * s))
                    pool.dma_start(v_in[s], vl[ds(i, 1), s].rearrange("a p n -> (a p) n")).then_inc(v_loaded[s], DMA)

            def norm_constants(n):
                for k, src in enumerate((ln_g, ln_b)):
                    pool.dma_start(gb[:, k * D:(k + 1) * D],
                                   src[n // 2, n % 2:n % 2 + 1].to_broadcast([P, D])).then_inc(gb_in, DMA)
                nc.gpsimd.memset(v_half, -0.5).then_inc(pool_step, ONE)
                pool.wait_ge(pool_step, 3 + (TT + 1) * n)
                for t in range(TT):
                    pool.wait_ge(ln_mean, TT * n + t + 1)
                    nc.gpsimd.tensor_scalar(ln_rstd[:, t:t + 1], ln_mv[:, t, 1:2], EPS, None, ALU.add).then_inc(pool_step, ONE)
                    pool.wait_ge(pool_step, 3 + (TT + 1) * n + t + 1)
                    nc.gpsimd.tensor_tensor(ln_rstd[:, t:t + 1], ln_rstd[:, t:t + 1], v_half[:, 0:1], ALU.pow
                                            ).then_inc(ln_scale, ONE)

            norm_constants(0)
            wait_turned(pool, 1)
            norm_constants(1)
            wait_turned(pool, 2)
            nc.gpsimd.memset(bias[2], BIG).then_inc(bias_clear, ONE)
            for k in range(4):
                pool.wait_ge(up_free[k % 2], freed(V2.up, k // 2))
                u, q = k // 2, k % 2
                dst = vnat_dram.rearrange("(q t p) (u n) -> q u p t n", q=2, t=4, u=2)[q, u]
                pool.dma_start(dst, tmp[k].rearrange("p (t n) -> p t n", t=4)).then_inc(attn_v_stored, DMA)
            pool.wait_ge(attn_v_stored, 4 * DMA)
            pool.wait_ge(bias_clear, 1)
            pool.wait_ge(skew_stored, 3 * DMA)
            v_tok = [vnat_dram.rearrange("(t p) (i c) -> i p t c", p=P, i=NPAIR),
                     vnat_dram.rearrange("(n p r) (i c) -> i r p n c", n=2, r=4, i=NPAIR),
                     vnat_dram.rearrange("(s t h) (i c) -> i h s t c", s=HD, h=2, i=NPAIR)]
            o_tok = [None, o_dram[0].rearrange("(n p r) c -> r p n c", n=2, r=4),
                     o_dram[1].rearrange("(s t h) c -> h s t c", s=HD, h=2)]

            def skewed(g, hh, at, n, w, i):
                sk = skew_dram[8 * g:8 * g + 8].rearrange("(i h) n -> i h n", h=2)[:, hh]
                v = sk[:, at:at + n * (TABW - 1)].rearrange("i (p w) -> i p w", w=TABW - 1)[:, :, 0:w]
                return v[ds(i, 1)].rearrange("a p w -> (a p) w")

            with pool.Fori(0, NPAIR) as i:
                d = AT.down + PAIR_DOWN * i
                wait_apart(pool, (down_done, d - TT))
                for h in range(2):
                    pool.dma_start(v_perm[0][h * HD:(h + 1) * HD],
                                   v_tok[2][ds(i, 1), h].rearrange("a s t c -> (a s) t c")).then_inc(vp_in[2], DMA)
                for hh in range(2):
                    for h in range(2):
                        pool.dma_start(bias[2][h * HD:(h + 1) * HD, hh, h * HD:(h + 1) * HD],
                                       skewed(2, hh, 255, HD, HD, i)).then_inc(bias_in[2], DMA)
                for hh in range(2):
                    pool.dma_start(bias[1][:, hh], skewed(1, hh, 127, P, 256, i)).then_inc(bias_in[1], DMA)
                for r in range(4):
                    pool.dma_start(v_perm[1][:, 2 * r:2 * r + 2],
                                   v_tok[1][ds(i, 1), r].rearrange("a p n c -> (a p) n c")).then_inc(vp_in[1], DMA)
                for hh in range(2):
                    pool.dma_start(bias[0][:, hh], skewed(0, hh, 127, P, 256, i)).then_inc(bias_in[0], DMA)
                wait_apart(pool, (down_done, d + 8))
                pool.dma_start(v_perm[0], v_tok[0][ds(i, 1)].rearrange("a p t c -> (a p) t c")).then_inc(vp_in[0], DMA)
                for g in (2, 1):
                    wait_apart(pool, *[(down_free[b], freed(AT.down + STEP_DOWN[g], 3) + PAIR_DOWN // 2 * i) for b in range(2)])
                    if g == 2:
                        for h in range(2):
                            pool.dma_start(o_tok[2][h], nat[2][h * HD:(h + 1) * HD]).then_inc(nat_stored[2], DMA)
                    else:
                        for r in range(4):
                            pool.dma_start(o_tok[1][r], nat[1][:, 2 * r:2 * r + 2]).then_inc(nat_stored[1], DMA)
                    stores = 2 if g == 2 else 4
                    wait_apart(pool, (nat_stored[g], stores * DMA * i + stores * DMA))
                    pool.dma_start(nat[g], o_dram[g - 1].rearrange("(t p) c -> p t c", p=P)).then_inc(nat_in[g], DMA)
            pool.wait_ge(o_done, NPAIR)
            norm_constants(2)
            wait_turned(pool, 3)
            norm_constants(3)

        @block.scalar
        def _(act):
            def hi_col(B, j, s, fills):
                act.wait_ge(col_in[s], DMA * (B.col // 2 + 1) + DMA * j)
                act.wait_ge(up_done, fills)
                nc.scalar.activation(col_hi[:, s], raw_col[:, s], ACT.Copy).then_inc(col_hi_done, ONE)

            def hi_wide(came, j, k, downs=None, fills=None):
                act.wait_ge(wide_in[k], DMA * (came + 1) + DMA * j)
                if downs is not None:
                    act.wait_ge(down_done, downs)
                if fills is not None:
                    act.wait_ge(up_done, fills)
                nc.scalar.activation(wide_hi[:, k], raw_wide[:, k], ACT.Copy).then_inc(wide_hi_done, ONE)

            for t in range(TT):
                act.wait_ge(down_done, X_DOWN + t + 1)
                nc.scalar.activation(xt_hi[:, :, t * P:(t + 1) * P], down[t % 2][:].rearrange("p (k t) -> p k t", k=KT),
                                     ACT.Copy).then_inc(xt_hi_done, ONE)
                nc.scalar.mul(res[:, t], res[:, t], ALPHA).then_inc(res_scaled, ONE)
            for s in range(2):
                hi_col(V1, 0, s, 1)
            act.wait_ge(up_done, SET_UP + 1)
            nc.scalar.copy(par[:, 0:4], up[0][:, 0:4 * P].rearrange("p (b n) -> p b n", b=4)[:, :, 0:88]).then_inc(up_free[0], ONE)
            act.wait_ge(up_done, SET_UP + 2)
            nc.scalar.copy(par[:, 4, 0:32], up[1][:, 0:32]).then_inc(up_free[1], ONE)
            act.wait_ge(up_done, SET_UP + 3)
            nc.scalar.copy(tab_rows[0:8, 0:2 * TABW].rearrange("p (g n) -> p g n", g=2),
                           up[0][0:8].rearrange("p (g n) -> p g n", g=2)[:, :, 0:TABW]).then_inc(up_free[0], ONE)
            act.wait_ge(up_done, SET_UP + 4)
            nc.scalar.copy(tab_rows[0:8, 2 * TABW:], up[1][0:8, 0:TABW]).then_inc(up_free[1], ONE)
            act.wait_ge(up_done, SET_UP + 5)
            nc.scalar.copy(ws_t, up[0][:]).then_inc(up_free[0], ONE)

            def v_tiles(i, u, first):
                for q in range(2):
                    k = 2 * u + q
                    act.wait_ge(up_done, V1.up + 4 * i + k + 1)
                    act.wait_ge(v_counted, 4 * i + k + 1)
                    if not first:
                        act.wait_ge(v_stored[k], 2 * DMA * i)
                    nc.scalar.activation(tmp[k], up[q][:], ACT.Gelu).then_inc(up_free[q], ONE)

            for start, end in ((0, 1), (1, 4)):
                with act.Fori(start, end) as i:
                    for k in range(2):
                        hi_wide(V1.in0, i, k, fills=V1.up + 4 * i)
                    v_tiles(i, 0, start == 0)
                    for s in range(2):
                        hi_col(V1, i + 1, s, V1.up + 4 * i + 2)
                    v_tiles(i, 1, start == 0)

            def hid_hi_part(B, i, s):
                act.wait_ge(y_done, B.hid + 2 * i + s + 3)
                act.wait_ge(down_done, B.down + TT * i)
                nc.scalar.activation(hid_hi[:, s], tmp[2 + s], ACT.Copy).then_inc(hid_hi_done, ONE)

            for k in range(4):
                act.wait_ge(v_stored[k], 8 * DMA)
            with act.Fori(0, SG) as i:
                for s in range(2):
                    act.wait_ge(up_done, G1.up + 4 * i + 2 * s + 1)
                    act.wait_ge(y_done, G1.hid + 2 * i + s + 1)
                    nc.scalar.activation(tmp[s], up[0][:], ACT.Gelu).then_inc(up_free[0], ONE)
                    hi_col(G1, i + 1, s, G1.up + 4 * i + 2 * s + 1)
                    if s == 0:
                        for k in range(2):
                            hi_wide(G1.in0, i, k, downs=G1.down + TT * i)
                    hid_hi_part(G1, i, s)

            def ln_out(n):
                for t in range(TT):
                    act.wait_ge(down_done, LN_DOWN[n] + t + 1)
                    nc.scalar.activation(xt_hi[:, :, t * P:(t + 1) * P], down[t % 2][:].rearrange("p (k t) -> p k t", k=KT),
                                         ACT.Copy).then_inc(xt_hi_done, ONE)
                    nc.scalar.mul(res[:, t], tmp[t % 4], ALPHA).then_inc(res_scaled, ONE)
                act.wait_ge(res_scaled, TT * (n + 2))

            def ffn(l, B):
                def first_tap(i, q):
                    act.wait_ge(up_done, B.up + 4 * i + q + 1)
                    if q < 2:
                        act.wait_ge(y_done, B.hid + 2 * i + q + 1)
                    else:
                        act.wait_ge(hid_ready, B.hid + 2 * i + q - 2 - 1)
                    nc.scalar.activation(tmp[q], up[q % 2][:], ACT.Identity, bias=tap(l, 3, q, i),
                                         scale=tap(l, 2, q, i)).then_inc(tap0_done, ONE)

                def chunk(i, split_next):
                    for q in range(4):
                        if q < 2 or split_next:
                            hi_col(B, 2 * i + 1 + q // 2, q % 2, B.up + 4 * i + q + 1)
                        first_tap(i, q)
                        if q < 2:
                            act.wait_ge(up_free[q], freed(B.up, 2 * i))
                            nc.scalar.activation(tmp[q], tmp[q], ACT.Gelu).then_inc(gate_act, ONE)
                        else:
                            hid_hi_part(B, i, q - 2)
                        if q == 1:
                            for k in range(2):
                                hi_wide(B.in0 if k == 0 else B.in1, i, k, downs=B.down + TT * i)

                with act.Fori(0, FI - 1) as i:
                    chunk(i, True)
                with act.Fori(FI - 1, FI) as i:
                    chunk(i, l == 0)

            ln_out(0)
            ffn(0, F1)
            ln_out(1)
            for k in range(2):
                hi_wide(V2.in0 if k == 0 else V2.in1, 0, k, downs=V2.down)
            for k in range(4):
                act.wait_ge(up_done, V2.up + k + 1)
                nc.scalar.copy(tmp[k], up[k % 2][:]).then_inc(up_free[k % 2], ONE)
                if k == 1:
                    for s in range(2):
                        hi_col(AT, 0, s, V2.up + 2)
            act.wait_ge(attn_v_stored, 4 * DMA)
            q_scale = -HD ** -0.5
            act.wait_ge(up_done, AT.up + 1)
            nc.scalar.copy(k_t, up[0][:]).then_inc(up_free[0], ONE)
            with act.Fori(0, 1) as i:
                hi_col(AT, i + 1, 0, AT.up + 1)
            act.wait_ge(up_done, AT.up + 2)
            nc.scalar.mul(q_t[1], up[1][:], q_scale).then_inc(up_free[1], ONE)
            with act.Fori(0, 1) as i:
                hi_col(AT, i + 1, 1, AT.up + 2)

            def group2_queries(fills):
                act.wait_ge(up_done, fills)
                nc.scalar.mul(q_t[0].rearrange("p (t h s) -> p t h s", t=8, h=2),
                              up[0][:].rearrange("p (s t h) -> p t h s", t=8, h=2), q_scale).then_inc(up_free[0], ONE)

            def pair(i, last):
                m = AT.up + PAIR_UP * i
                m2 = PAIR_UP // 2 * i
                d = AT.down + PAIR_DOWN * i
                hi_col(AT, 2 * i + 2, 0, m + Q2_UP + 1)
                for k in range(24 + 3):
                    if k == 4:
                        act.wait_ge(wide_in[0], DMA * (AT.in0 + 1) + DMA * i)
                        act.wait_ge(down_done, d)
                        nc.scalar.activation(wide_hi[:, 0], raw_wide[:, 0], ACT.Copy).then_inc(wide_hi_done, ONE)
                    if k == 8:
                        act.wait_ge(up_done, m + Q0_UP + 1)
                        nc.scalar.mul(q_t[0], up[1][:], q_scale).then_inc(up_free[1], ONE)
                        hi_col(AT, 2 * i + 2, 1, m + Q0_UP + 1)
                    if k < 24:
                        g, t, keys, w = steps()[k]
                        p = prob[k % 4]
                        f = step_up(k)
                        for h in range(2):
                            if h == 0:
                                act.wait_ge(logits_a, 24 * i + k + 1)
                            else:
                                act.wait_ge(up_free[f % 2], freed(AT.up + f - f % 2, 0) + m2)
                            e = nc.scalar.activation(p[:, h, 0:w], p[:, h, 0:w], ACT.Exp, scale=-1.0,
                                                     bias=nat[g][:, t, 2 * HD + h:2 * HD + h + 1],
                                                     accum_out=nat[g][:, t, 2 * HD + 2 + h:2 * HD + 3 + h])
                        e.then_inc(exp_done, ONE)
                    if k >= 3:
                        g, t, _, _ = steps()[k - 3]
                        b = (k - 3) % 2
                        act.wait_ge(down_done, d + k - 3 + 1)
                        nc.scalar.copy(nat[g][:, t, 0:2 * HD], down[b][:, HALF:HALF + 2 * HD]).then_inc(down_free[b], ONE)
                act.wait_ge(mix_delta, i + 1)
                nc.scalar.activation(mix[:, 16:64], mix[:, 16:64], ACT.Exp).then_inc(mix_exp, ONE)
                turned_up = NEXT_UP
                if not last:
                    act.wait_ge(up_done, m + NEXT_UP + 1)
                    nc.scalar.copy(k_t, up[0][:]).then_inc(up_free[0], ONE)
                    hi_col(AT, 2 * i + 3, 0, m + NEXT_UP + 1)
                    act.wait_ge(up_done, m + NEXT_UP + 2)
                    nc.scalar.mul(q_t[1], up[1][:], q_scale).then_inc(up_free[1], ONE)
                    hi_col(AT, 2 * i + 3, 1, m + NEXT_UP + 2)
                    turned_up += 2
                for b in range(2):
                    act.wait_ge(up_done, m + turned_up + b + 1)
                    act.wait_ge(down_done, d)
                    nc.scalar.activation(hid_hi[:, 0, b * HALF:(b + 1) * HALF], up[b][:, 0:HALF], ACT.Copy).then_inc(o_hi_done, ONE)
                if not last:
                    group2_queries(m + PAIR_UP + Q2_UP + 1)

            group2_queries(AT.up + Q2_UP + 1)
            with act.Fori(0, NPAIR - 1) as i:
                pair(i, False)
            with act.Fori(NPAIR - 1, NPAIR) as i:
                pair(i, True)
            ln_out(2)
            ffn(1, F2)

        @block.vector
        def _(dve):
            dve.sem_inc(col_lo_done, 2)
            dve.sem_inc(wide_lo_done, 2)
            dve.sem_inc(v_counted, 4)
            dve.sem_inc(y_done, 2)

            def lo_col(B, j, s):
                dve.wait_ge(col_hi_done, B.col + 2 * j + s + 1)
                nc.vector.tensor_tensor(col_lo[:, s], raw_col[:, s], col_hi[:, s], ALU.subtract).then_inc(col_lo_done, ONE)

            def lo_wide(n, k):
                dve.wait_ge(wide_hi_done, n + 1)
                nc.vector.tensor_tensor(wide_lo[:, k], raw_wide[:, k], wide_hi[:, k], ALU.subtract).then_inc(wide_lo_done, ONE)

            def turned_lo(n, at, t):
                dve.wait_ge(xt_hi_done, TT * n + t + 1)
                tk = slice(t * P, (t + 1) * P)
                nc.vector.tensor_tensor(xt_lo[:, :, tk], down[t % 2][:].rearrange("p (k t) -> p k t", k=KT),
                                        xt_hi[:, :, tk], ALU.subtract).then_inc(down_free[t % 2], ONE)

            def add_down(at):
                for t in range(TT):
                    dve.wait_ge(down_done, at + t + 1)
                    nc.vector.tensor_tensor(res[:, t], down[t % 2][:], res[:, t], ALU.add).then_inc(down_free[t % 2], ONE)

            for t in range(TT):
                turned_lo(0, X_DOWN, t)
            dve.wait_ge(res_scaled, TT)
            for s in range(2):
                lo_col(V1, 0, s)
            dve.wait_ge(bs_in, DMA)
            dve.wait_ge(tab_stored, 3 * DMA)
            dve.wait_ge(up_free[1], freed(SET_UP, 0))
            dve.wait_ge(up_done, SET_UP + 6)
            for c in range(CT):
                g = c // 2
                last = nc.vector.scalar_tensor_tensor(out=bias_ts[:, c], in0=up[1][:, g * P:(g + 1) * P],
                                                      scalar=par[:, 4, CT + c:CT + c + 1], in1=bs_rows[:, g * P:(g + 1) * P],
                                                      op0=ALU.mult, op1=ALU.add)
            last.then_inc(up_free[1], ONE)

            def count_v(i, u):
                for q in range(2):
                    dve.wait_ge(up_free[q], freed(V1.up, u) + 2 * i)
                    for t in range(4):
                        last = nc.vector.bn_stats(v_stats.rearrange("p t (i u) x -> p t i u x", u=2)[:, 4 * q + t, ds(i, 1), u]
                                                  .rearrange("p a x -> p (a x)"),
                                                  tmp[2 * u + q][:, t * 2 * P:(t + 1) * 2 * P])
                    last.then_inc(v_counted, ONE)

            with dve.Fori(0, 4) as i:
                for k in range(2):
                    lo_wide(V1.wide + 2 * i + k, k)
                count_v(i, 0)
                for s in range(2):
                    lo_col(V1, i + 1, s)
                count_v(i, 1)
            dve.wait_ge(v_counted, 4 + 16)
            for t in range(TT):
                nc.vector.bn_aggr(v_mv[:, t], v_stats[:, t].rearrange("p j x -> p (j x)")).then_inc(v_mean, ONE)

            def hid_lo_part(B, i, s):
                dve.wait_ge(hid_hi_done, B.hid + 2 * i + s + 1)
                nc.vector.tensor_tensor(hid_lo[:, s], tmp[2 + s], hid_hi[:, s], ALU.subtract).then_inc(hid_ready, ONE)

            def normalize_v(i, s):
                dve.wait_ge(v_loaded[s], DMA * i + DMA)
                for t in range(TT):
                    last = nc.vector.tensor_scalar(v_in[s][:, t * P:(t + 1) * P], v_in[s][:, t * P:(t + 1) * P],
                                                   v_mv[:, t, 0:1], v_rstd[:, t:t + 1], ALU.subtract, ALU.mult)
                last.then_inc(v_norm, ONE)

            def layer_norm(n, down_at, turn):
                def add_and_count(t):
                    b = t % 2
                    dve.wait_ge(down_done, down_at + t + 1)
                    nc.vector.tensor_tensor(res[:, t], down[b][:], res[:, t], ALU.add).then_inc(down_free[b], ONE)
                    dve.wait_ge(down_free[b], freed(down_at, t // 2))
                    for j in range(2):
                        last = nc.vector.bn_stats(ln_stats[:, t, j], res[:, t, j * HALF:(j + 1) * HALF])
                    last.then_inc(ln_counted, ONE)
                    dve.wait_ge(ln_counted, TT * n + t + 1)
                    nc.vector.bn_aggr(ln_mv[:, t], ln_stats[:, t].rearrange("p j x -> p (j x)")).then_inc(ln_mean, ONE)

                def normalize(u):
                    xn = tmp[u % 4]
                    if u == 0:
                        dve.wait_ge(gb_in, 2 * DMA * (n + 1))
                    if u >= 4 and turn:
                        dve.wait_ge(res_scaled, TT * (n + 1) + u - 3)
                    if u >= 4 and not turn:
                        dve.wait_ge(out_stored[u % 4], DMA)
                    dve.wait_ge(ln_mean, TT * n + u + 1)
                    nc.vector.scalar_tensor_tensor(out=xn, in0=res[:, u], scalar=ln_mv[:, u, 0:1], in1=gb[:, 0:D],
                                                   op0=ALU.subtract, op1=ALU.mult).then_inc(ln_step, ONE)
                    dve.wait_ge(ln_step, TT * n + u + 1)
                    dve.wait_ge(ln_scale, TT * n + u + 1)
                    nc.vector.scalar_tensor_tensor(out=xn, in0=xn, scalar=ln_rstd[:, u:u + 1], in1=gb[:, D:2 * D],
                                                   op0=ALU.mult, op1=ALU.add).then_inc(xn_done, ONE)

                ahead = 4 if turn else TT
                for t in range(TT):
                    add_and_count(t)
                    if 1 <= t <= ahead:
                        normalize(t - 1)
                if not turn:
                    normalize(TT - 1)
                else:
                    for t in range(TT):
                        turned_lo(n + 1, LN_DOWN[n], t)
                        if 1 <= t <= 4:
                            normalize(t + 3)
                    dve.wait_ge(res_scaled, TT * (n + 2))

            def gated(i, last_group):
                for s in range(2):
                    lo_col(G1, i + 1, s)
                    if s == 0:
                        for k in range(2):
                            lo_wide(G1.wide + 2 * i + k, k)
                    dve.wait_ge(up_done, G1.up + 4 * i + 2 * s + 2)
                    gain = par[:, 4, 0:CT].rearrange("p (i s) -> p i s", s=2)[:, ds(i, 1), s]
                    term = bias_ts.rearrange("p (i s) t -> p i s t", s=2)[:, ds(i, 1), s].to_broadcast([P, TT, P])
                    nc.vector.scalar_tensor_tensor(out=tmp[2 + s].rearrange("p (t n) -> p t n", t=TT),
                                                   in0=up[1][:].rearrange("p (t n) -> p t n", t=TT), scalar=gain,
                                                   in1=term, op0=ALU.mult, op1=ALU.add).then_inc(up_free[1], ONE)
                    dve.wait_ge(up_free[1], freed(G1.up, s) + 2 * i)
                    dve.wait_ge(up_free[0], freed(G1.up, s) + 2 * i)
                    nc.vector.tensor_tensor(tmp[2 + s], tmp[2 + s], tmp[s], ALU.mult).then_inc(y_done, ONE)
                    hid_lo_part(G1, i, s)
                    if not last_group:
                        normalize_v(i + 1, s)
                if not last_group:
                    add_down(G1.down + TT * i)

            dve.wait_ge(v_scale, 1)
            dve.wait_ge(v_mean, TT)
            for s in range(2):
                normalize_v(0, s)
            with dve.Fori(0, SG - 1) as i:
                gated(i, False)
            with dve.Fori(SG - 1, SG) as i:
                gated(i, True)
            layer_norm(0, LN_DOWN[0] - TT, True)

            def ffn(l, B):
                def other_taps(i, q):
                    dve.wait_ge(tap0_done, B.tap + 4 * i + q + 1)
                    b = q % 2
                    nc.vector.scalar_tensor_tensor(out=tmp[q][:, 1:T], in0=up[b][:, 0:T - 1], scalar=tap(l, 1, q, i),
                                                   in1=tmp[q][:, 1:T], op0=ALU.mult, op1=ALU.add).then_inc(tap1_done, ONE)
                    dve.wait_ge(tap1_done, B.tap + 4 * i + q + 1)
                    nc.vector.scalar_tensor_tensor(out=tmp[q][:, 2:T], in0=up[b][:, 0:T - 2], scalar=tap(l, 0, q, i),
                                                   in1=tmp[q][:, 2:T], op0=ALU.mult, op1=ALU.add).then_inc(up_free[b], ONE)

                def chunk(i, split_next):
                    for q in range(4):
                        if q < 2 or split_next:
                            lo_col(B, 2 * i + 1 + q // 2, q % 2)
                        other_taps(i, q)
                        if q >= 2:
                            s = q - 2
                            dve.wait_ge(up_free[s], freed(B.up, 1) + 2 * i)
                            dve.wait_ge(gate_act, B.tap // 2 + 2 * i + s + 1)
                            nc.vector.tensor_tensor(tmp[q], tmp[q], tmp[s], ALU.mult).then_inc(y_done, ONE)
                            hid_lo_part(B, i, s)
                        if q == 1:
                            for k in range(2):
                                lo_wide(B.wide + 2 * i + k, k)

                with dve.Fori(0, FI - 1) as i:
                    chunk(i, True)
                    add_down(B.down + TT * i)
                with dve.Fori(FI - 1, FI) as i:
                    chunk(i, l == 0)

            ffn(0, F1)
            layer_norm(1, LN_DOWN[1] - TT, True)
            for k in range(2):
                lo_wide(V2.wide + k, k)
            for s in range(2):
                lo_col(AT, 0, s)
            dve.wait_ge(attn_v_stored, 4 * DMA)
            def mix_groups(i):
                MIX = 11
                count = [0]

                def link(ins):
                    ins.then_inc(mix_step, ONE)
                    count[0] += 1
                    dve.wait_ge(mix_step, MIX * i + count[0])

                for g in (1, 2):
                    dve.wait_ge(nat_in[g], DMA * i + DMA)
                for b in range(2):
                    dve.wait_ge(down_free[b], freed(AT.down + STEP_DOWN[0], 3) + PAIR_DOWN // 2 * i)

                def stat(g, at):
                    return nat[g][:, :, 2 * HD + at:2 * HD + at + 2]

                def small(n):
                    return mix[:, 16 * n:16 * n + 16].rearrange("p (t h) -> p t h", t=TT)

                tt = nc.vector.tensor_tensor
                link(tt(small(0), stat(0, 0), stat(1, 0), ALU.min))
                link(tt(small(0), small(0), stat(2, 0), ALU.min))
                for g in range(3):
                    last = tt(small(1 + g), small(0), stat(g, 0), ALU.subtract)
                last.then_inc(mix_delta, ONE)
                dve.wait_ge(mix_exp, i + 1)
                for g in range(3):
                    last = tt(small(4 + g), small(1 + g), stat(g, 2), ALU.mult)
                link(last)
                link(tt(small(4), small(4), small(5), ALU.add))
                link(tt(small(4), small(4), small(6), ALU.add))
                link(nc.vector.reciprocal(small(7), small(4)))
                for g in range(3):
                    last = tt(small(1 + g), small(1 + g), small(7), ALU.mult)
                link(last)
                for g in range(3):
                    v = nat[g][:, :, 0:2 * HD].rearrange("p t (h d) -> p t h d", h=2)
                    wb = small(1 + g).rearrange("p t (h o) -> p t h o", o=1).to_broadcast([P, TT, 2, HD])
                    link(tt(v, v, wb, ALU.mult))
                o = q_t[0].rearrange("p (t c) -> p t c", t=TT)
                link(tt(o, nat[0][:, :, 0:2 * HD], nat[1][:, :, 0:2 * HD], ALU.add))
                tt(o, o, nat[2][:, :, 0:2 * HD], ALU.add).then_inc(o_done, ONE)

            def pair(i, last):
                lo_col(AT, 2 * i + 2, 0)
                for k in range(24 + 2):
                    if k == 4:
                        lo_wide(AT.wide + i, 0)
                    if k == 8:
                        lo_col(AT, 2 * i + 2, 1)
                    if k < 24:
                        g, t, keys, w = steps()[k]
                        if t == 0:
                            dve.wait_ge(bias_in[g], (4 if g == 2 else 2) * DMA * (i + 1))
                        f = step_up(k)
                        wait_apart(dve, (up_done, AT.up + PAIR_UP * i + f + 1))
                        for h in range(2):
                            nc.vector.tensor_tensor_reduce(prob[k % 4][:, h, 0:w], up[f % 2][:, h * HALF:h * HALF + w],
                                                           bias[g][:, h, b_w[g] - w:b_w[g]], 1.0, 3e38, ALU.add, ALU.min,
                                                           nat[g][:, t, 2 * HD + h:2 * HD + h + 1]
                                                           ).then_inc(up_free[f % 2] if h else logits_a, ONE)
                    if k >= 2:
                        j = k - 2
                        w = steps()[j][3]
                        dve.wait_ge(turned, 24 * i + j + 1)
                        dve.wait_ge(down_done, AT.down + PAIR_DOWN * i + j - 1)
                        nc.vector.tensor_copy(prob_t[j % 2][:, :, 0:w],
                                              down[j % 2][:, 0:HALF].rearrange("p (h w) -> p h w", h=2)[:, :, 0:w]
                                              ).then_inc(prob_t_ready, ONE)
                mix_groups(i)
                if not last:
                    for s in range(2):
                        lo_col(AT, 2 * i + 3, s)
                for b in range(2):
                    dve.wait_ge(o_hi_done, 2 * i + b + 1)
                    nc.vector.tensor_tensor(hid_lo[:, 0, b * HALF:(b + 1) * HALF], up[b][:, 0:HALF], hid_hi[:, 0, b * HALF:(b + 1) * HALF],
                       ALU.subtract).then_inc(up_free[b], ONE)
                if not last:
                    add_down(AT.down + PAIR_DOWN * i + 24)

            with dve.Fori(0, 1) as i:
                for s in range(2):
                    lo_col(AT, i + 1, s)
            with dve.Fori(0, NPAIR - 1) as i:
                pair(i, False)
            with dve.Fori(NPAIR - 1, NPAIR) as i:
                pair(i, True)
            layer_norm(2, LN_DOWN[2] - TT, True)
            ffn(1, F2)
            layer_norm(3, LN_DOWN[3] - TT, False)

        @block.tensor
        def _(pe):
            for b in range(2):
                pe.sem_inc(up_free[b], 1)
                pe.sem_inc(down_free[b], X_DOWN // 2 + 1)
            pe.sem_inc(down_done, X_DOWN)

            def mm(o, a, b, start, stop, **kw):
                return nc.tensor.matmul(o, a, b, start=start, stop=stop, **kw)

            def split_mm(o, a, b, first, last):
                mm(o, a[0], b[0], first, False)
                mm(o, a[0], b[1], False, False)
                return mm(o, a[1], b[0], False, last)

            def up_free_for(at, j):
                pe.wait_ge(up_free[at % 2], at // 2 + 1 + j)

            def turn(at, t, tile):
                pe.wait_ge(down_free[t % 2], (at + t) // 2 + 1)
                for k in range(KT):
                    last = nc.tensor.transpose(down[t % 2][:, k * P:(k + 1) * P], tile[:, k * P:(k + 1) * P], ident[:])
                last.then_inc(down_done, ONE)

            def turn_xn(n, tiles):
                for t in tiles:
                    pe.wait_ge(xn_done, TT * n + t + 1)
                    turn(LN_DOWN[n], t, tmp[t % 4])

            def features(at, j, piece, s, halves=(0, 1)):
                if halves[0] == 0:
                    pe.wait_ge(col_lo_done, piece + 3)
                    up_free_for(at, j)
                for h in halves:
                    for k in range(KT):
                        sl = slice(h * HALF, (h + 1) * HALF)
                        last = split_mm(up[at % 2][:, sl], (col_hi[:, s, k], col_lo[:, s, k]),
                                        (xt_hi[:, k, sl], xt_lo[:, k, sl]), k == 0, k == KT - 1)
                if halves[-1] == 1:
                    last.then_inc(up_done, ONE)

            def down_unit(at, j, nk):
                for t in range(TT):
                    b = t % 2
                    pe.wait_ge(down_free[b], at // 2 + t // 2 + 1 + j)
                    for n in range(2):
                        sl = slice(n * HALF, (n + 1) * HALF)
                        tk = slice(t * P, (t + 1) * P)
                        for k in range(nk):
                            last = split_mm(down[b][:, sl], (hid_hi[:, k, tk], hid_lo[:, k, tk]),
                                            (wide_hi[:, k, sl], wide_lo[:, k, sl]), k == 0, k == nk - 1)
                    last.then_inc(down_done, ONE)

            def v_half(at, j, q, hi, lo):
                up_free_for(at + q, j)
                for t in range(4):
                    tk = slice((4 * q + t) * P, (4 * q + t + 1) * P)
                    o = up[q][:, t * 2 * P:(t + 1) * 2 * P].rearrange("p (s n) -> p s n", s=2)
                    for k in range(KT):
                        last = split_mm(o, (xt_hi[:, k, tk], xt_lo[:, k, tk]), (hi[:, :, k], lo[:, :, k]),
                                        k == 0, k == KT - 1)
                last.then_inc(up_done, ONE)

            pe.wait_ge(ident_in, DMA)
            for t in range(TT):
                pe.wait_ge(x_in[t], DMA)
                turn(X_DOWN, t, res[:, t])
            pe.wait_ge(par_in, 10 * DMA)
            up_free_for(SET_UP, 0)
            for blk in range(4):
                last = nc.tensor.transpose(up[0][:, blk * P:blk * P + 88], tmp[2][0:88, blk * P:(blk + 1) * P], ident[0:88, 0:88])
            last.then_inc(up_done, ONE)
            up_free_for(SET_UP + 1, 0)
            nc.tensor.transpose(up[1][:, 0:32], tmp[2][0:32, 4 * P:5 * P], ident[0:32, 0:32]).then_inc(up_done, ONE)
            pe.wait_ge(tab_in, 2 * DMA)
            pe.wait_ge(consts_ready, 2)
            up_free_for(SET_UP + 2, 0)
            for g in range(2):
                last = mm(up[0][0:8, g * HALF:g * HALF + TABW], table[0:33, 8 * g:8 * g + 8],
                          pick[0:33, g * TABW:(g + 1) * TABW], True, True)
            last.then_inc(up_done, ONE)
            up_free_for(SET_UP + 3, 0)
            mm(up[1][0:8, 0:TABW], table[0:33, 16:24], pick[0:33, 2 * TABW:3 * TABW], True, True).then_inc(up_done, ONE)
            pe.wait_ge(ws_masked, 1)
            up_free_for(SET_UP + 4, 0)
            for g in range(SG):
                last = nc.tensor.transpose(up[0][:, g * P:(g + 1) * P], ws_t[:, g * P:(g + 1) * P], ident[:])
            last.then_inc(up_done, ONE)
            pe.wait_ge(up_free[0], freed(SET_UP, 2))
            up_free_for(SET_UP + 5, 0)
            for h in range(2):
                last = mm(up[1][:, h * HALF:(h + 1) * HALF], ones, ws_t[:, h * HALF:(h + 1) * HALF], True, True)
            last.then_inc(up_done, ONE)

            wait_turned(pe, 0)
            with pe.Fori(0, 4) as i:
                pe.wait_ge(col_lo_done, V1.col + 2 * i + 4)
                for q in range(2):
                    v_half(V1.up, 2 * i, q, col_hi, col_lo)
                pe.wait_ge(wide_lo_done, V1.wide + 2 * i + 4)
                for q in range(2):
                    v_half(V1.up + 2, 2 * i, q, wide_k_hi, wide_k_lo)

            def mixed(i, s):
                pe.wait_ge(v_norm, 2 * i + s + 1)
                up_free_for(G1.up + 2 * s + 1, 2 * i)
                for t in range(TT):
                    last = mm(up[1][:, t * P:(t + 1) * P], v_in[s][:, t * P:(t + 1) * P],
                              ws_t.rearrange("p (g t) -> p g t", g=SG)[:, ds(i, 1)].rearrange("p a t -> p (a t)"), True, True)
                last.then_inc(up_done, ONE)

            def gated(i, last_group):
                mixed(i, 0)
                features(G1.up + 2, 2 * i, G1.col + 2 * i + 1, 1)
                mixed(i, 1)
                if not last_group:
                    features(G1.up + 4, 2 * i, G1.col + 2 * i + 2, 0)
                pe.wait_ge(hid_ready, G1.hid + 2 * i + 2)
                pe.wait_ge(wide_lo_done, G1.wide + 2 * i + 4)
                down_unit(G1.down, 4 * i, 2)

            features(G1.up, 0, G1.col, 0)
            with pe.Fori(0, SG - 1) as i:
                gated(i, False)
            with pe.Fori(SG - 1, SG) as i:
                gated(i, True)

            def ffn(B, n):
                def chunk(i, last_chunk):
                    for q in range(2, 4):
                        features(B.up + q, 2 * i, B.col + 4 * i + q, q % 2)
                    if not last_chunk:
                        features(B.up + 4, 2 * i, B.col + 4 * i + 4, 0)
                    pe.wait_ge(hid_ready, B.hid + 2 * i + 2)
                    pe.wait_ge(wide_lo_done, B.wide + 2 * i + 4)
                    down_unit(B.down, 4 * i, 2)
                    if not last_chunk:
                        features(B.up + 5, 2 * i, B.col + 4 * i + 5, 1)

                turn_xn(n, range(0, 5))
                wait_turned(pe, n + 1, 4)
                features(B.up, 0, B.col, 0, (0,))
                turn_xn(n, [5])
                features(B.up + 1, 0, B.col + 1, 1, (0,))
                turn_xn(n, [6, 7])
                wait_turned(pe, n + 1)
                features(B.up, 0, B.col, 0, (1,))
                features(B.up + 1, 0, B.col + 1, 1, (1,))
                with pe.Fori(0, FI - 1) as i:
                    chunk(i, False)
                with pe.Fori(FI - 1, FI) as i:
                    chunk(i, True)

            ffn(F1, 0)
            pe.wait_ge(col_lo_done, V2.col + 4)
            turn_xn(1, range(0, 5))
            wait_turned(pe, 2, 4)
            v_half(V2.up, 0, 0, col_hi, col_lo)
            turn_xn(1, range(5, TT))
            wait_turned(pe, 2)
            v_half(V2.up, 0, 1, col_hi, col_lo)
            pe.wait_ge(wide_lo_done, V2.wide + 4)
            for q in range(2):
                v_half(V2.up + 2, 0, q, wide_k_hi, wide_k_lo)

            def pair(i, last_pair):
                m2 = PAIR_UP // 2 * i
                d2 = PAIR_DOWN // 2 * i
                st = steps()
                pe.wait_ge(up_free[0], freed(AT.up + Q2_UP, 0) + m2)
                for k in range(24 + 3):
                    if k == 16:
                        pe.wait_ge(up_free[1], freed(AT.up + Q0_UP - 1, 0) + m2)
                    if k < 24:
                        g, t, keys, w = st[k]
                        q = q_t[1 if g == 1 else 0]
                        f = step_up(k)
                        up_free_for(AT.up + f, m2)
                        for h in range(2):
                            hp = slice(h * HD, (h + 1) * HD)
                            queries = q[hp, t * P:(t + 1) * P] if g == 2 else tokens(q[hp], g, t, 1)
                            last = mm(up[f % 2][:, h * HALF:h * HALF + w], queries,
                                      tokens(k_t[hp], g, t, len(keys)), True, True)
                        last.then_inc(up_done, ONE)
                    if 2 <= k < 26:
                        j = k - 2
                        pe.wait_ge(exp_done, 24 * i + j + 1)
                        pe.wait_ge(down_free[j % 2], (AT.down + j) // 2 + 1 + d2)
                        for h in range(2):
                            for c in range(len(st[j][2])):
                                last = nc.tensor.transpose(down[j % 2][:, h * 2 * P + c * P:h * 2 * P + (c + 1) * P],
                                                           prob[j % 4][:, h, c * P:(c + 1) * P], ident[:])
                        last.then_inc(turned, ONE)
                    if k >= 3:
                        j = k - 3
                        g, t, keys, w = st[j]
                        if t == 0:
                            pe.wait_ge(vp_in[g], {2: 2, 1: 4, 0: 1}[g] * DMA * (i + 1))
                        pe.wait_ge(prob_t_ready, 24 * i + j + 1)
                        v = v_perm[1 if g == 1 else 0]
                        for h in range(2):
                            for c, kt in enumerate(keys):
                                last = mm(down[j % 2][:, HALF + h * HD:HALF + (h + 1) * HD],
                                          prob_t[j % 2][:, h, c * P:(c + 1) * P], v[:, kt, h * HD:(h + 1) * HD],
                                          c == 0, c == len(keys) - 1)
                        last.then_inc(down_done, ONE)
                    if k == 7:
                        features(AT.up + Q0_UP, m2, AT.col + 4 * i + 3, 1)
                turned_up = NEXT_UP
                if not last_pair:
                    features(AT.up + NEXT_UP, m2, AT.col + 4 * i + 4, 0)
                    features(AT.up + NEXT_UP + 1, m2, AT.col + 4 * i + 5, 1)
                    turned_up += 2
                pe.wait_ge(o_done, i + 1)
                for b in range(2):
                    up_free_for(AT.up + turned_up + b, m2)
                    for t in range(4):
                        c = (4 * b + t) * P
                        last = nc.tensor.transpose(up[b][:, t * P:(t + 1) * P], q_t[0][:, c:c + P], ident[:])
                    last.then_inc(up_done, ONE)
                if not last_pair:
                    features(AT.up + PAIR_UP + Q2_UP, m2, AT.col + 4 * i + 6, 0)
                for b in range(2):
                    pe.wait_ge(up_free[b], freed(AT.up + turned_up, 0) + m2)
                pe.wait_ge(wide_lo_done, AT.wide + i + 3)
                down_unit(AT.down + 24, PAIR_DOWN // 2 * i, 1)

            for f in range(3):
                features(AT.up + f, 0, AT.col + f, f % 2)
            with pe.Fori(0, NPAIR - 1) as i:
                pair(i, False)
            with pe.Fori(NPAIR - 1, NPAIR) as i:
                pair(i, True)
            ffn(F2, 2)


_INS = ['x', 'a_w_in', 'a_ln_g', 'a_ln_b', 'a_w_s', 'a_b_s', 'a_w_out', 'kv_w', 'b_w_q', 'b_w_o', 'rel_table',
        'ffn_w_up', 'ffn_conv_w', 'ffn_conv_b', 'ffn_w_down', 'ln_g', 'ln_b']
_OUT = (1, T, D)


def bucket_pick_constant():
    import numpy as np
    pick = np.zeros((33, len(DIL), TABW), np.float32)
    for g, dil in enumerate(DIL):
        for j in range(TABW):
            delta = 255 - j
            if not 0 <= delta <= 128:
                pick[32, g, j] = 1.0
                continue
            n = delta * dil
            bucket = n
            if n >= 16:
                scaled = np.log(np.float32(n) / np.float32(16)) / np.float32(np.log(2048 / 16)) * np.float32(16)
                bucket = min(16 + int(np.float32(scaled)), 31)
            pick[bucket, g, j] = -1.0
    return pick.reshape(33, len(DIL) * TABW)


def kernel(**inputs):
    import numpy as _np
    import concourse.bacc as _bacc
    from concourse import mybir as _mybir
    from concourse.bass_utils import run_bass_kernel_spmd as _run

    nc = _bacc.Bacc("TRN2", target_bir_lowering=False, num_devices=1)
    arrays, args = {}, []

    def give(name, a):
        arrays[f"in_{name}_dram"] = a
        args.append(nc.dram_tensor(f"in_{name}_dram", a.shape, _mybir.dt.from_np(a.dtype), kind="ExternalInput").ap())

    for name in _INS:
        give(name, _np.ascontiguousarray(inputs[name]))
    give("bucket_pick", bucket_pick_constant())
    give("identity", _np.eye(P, dtype=_np.float32))
    args.append(nc.dram_tensor("out_0_dram", _OUT, _mybir.dt.float32, kind="ExternalOutput").ap())
    program(nc, *args)
    r = _run(nc, [arrays], core_ids=[0])
    return r.results[0]["out_0_dram"]
```

```python
from contextlib import ExitStack

import concourse.bass as bass
from concourse import mybir

F32 = mybir.dt.float32
F32R = mybir.dt.float32r
ACT = mybir.ActivationFunctionType
ALU = mybir.AluOpType
ds = bass.ds

P = 128
T = 1024
D = 1024
KT = D // P
TT = T // P
HALF = 512
W_SGU = 2048
CT = W_SGU // P
SG = 8
D_FF = 2816
FT = D_FF // P
FI = FT // 2
HD = 64
NPAIR = 4
DIL = (1, 4, 16)
TABW = 384
ROW = 2 * HD + 4
ALPHA = 4 ** 0.25
EPS = 1e-5
BIG = 1e30
EARLY = 5
ONE = 1
DMA = 16


def program(nc, x, a_w_in, a_ln_g, a_ln_b, a_w_s, a_b_s, a_w_out, kv_w, b_w_q, b_w_o, rel_table,
            ffn_w_up, ffn_conv_w, ffn_conv_b, ffn_w_down, ln_g, ln_b, bucket_pick, identity, out):
    ctx = ExitStack()
    with ctx:
        def sb(name, shape, dt=F32):
            return ctx.enter_context(nc.sbuf_tensor(name, shape, dt))

        def sem(name):
            return ctx.enter_context(nc.semaphore(name))

        xt_hi = sb("xt_hi", [P, KT, T], F32R)
        xt_lo = sb("xt_lo", [P, KT, T], F32R)
        col_hi = sb("col_hi", [P, 2, KT, P], F32R)
        col_lo = sb("col_lo", [P, 2, KT, P], F32R)
        wide_hi = sb("wide_hi", [P, 2, D], F32R)
        wide_lo = sb("wide_lo", [P, 2, D], F32R)
        hid_hi = sb("hid_hi", [P, 2, T], F32R)
        hid_lo = sb("hid_lo", [P, 2, T], F32R)
        res = sb("res", [P, TT, D])
        raw_col = sb("raw_col", [P, 2, KT, P])
        raw_wide = sb("raw_wide", [P, 2, D])
        par = sb("par", [P, 5, 88])
        ident = sb("ident", [P, P])
        WORK = 11616
        work = sb("work", [P, WORK])

        def view(at, n):
            return work[:, at:at + n]

        tmp = [view(K * T, T) for K in range(4)]
        bias_ts = view(4096, 2048).rearrange("p (c t) -> p c t", c=CT)
        ws_t = view(6144, 1024)
        v_in = [view(7168 + s * 1024, 1024) for s in range(2)]
        bs_rows = view(7168, 1024)
        ones = view(8192, P)
        v_stats = view(9216, TT * 8 * 6).rearrange("p (t j x) -> p t j x", t=TT, j=8)
        gb = view(9216, 2 * D)
        v_mv = view(11264, 2 * TT).rearrange("p (t x) -> p t x", x=2)
        ln_mv = view(11280, 2 * TT).rearrange("p (t x) -> p t x", x=2)
        v_rstd = view(11296, TT)
        ln_rstd = view(11304, TT)
        v_half = view(11312, TT)
        ln_sum = view(11320, TT)
        squares = v_in[0]
        xn = tmp + [view(4096, T), view(5120, T), view(6144, T), v_in[1]]
        nat = [view(g * TT * ROW, TT * ROW).rearrange("p (t r) -> p t r", t=TT) for g in range(3)]
        k_t = view(3168, T)
        q_t = [view(4192 + s * T, T) for s in range(2)]
        v_perm = [view(6240 + s * T, T).rearrange("p (t c) -> p t c", t=TT) for s in range(2)]
        b_at = [8288, 8800, 9312]
        b_w = [256, 256, 128]
        bias = [view(b_at[g], 2 * b_w[g]).rearrange("p (h w) -> p h w", h=2) for g in range(3)]
        prob = [a.rearrange("p (h w) -> p h w", h=2)
                for a in (view(9568, 512), view(10080, 512), raw_wide[:, 1, 0:512], raw_wide[:, 1, 512:1024])]
        prob_t = [view(10592 + s * 512, 512).rearrange("p (h w) -> p h w", h=2) for s in range(2)]
        mix = view(9568, 160)
        table = view(9600, 24)
        pick = view(9632, 3 * TABW)
        tab_rows = view(4096, 3 * TABW)

        up = [ctx.enter_context(nc.psum_tensor(f"up{b}", [P, 2 * HALF], F32)) for b in range(2)]
        down = [ctx.enter_context(nc.psum_tensor(f"down{b}", [P, 2 * HALF], F32)) for b in range(2)]

        v_dram = nc.dram_tensor("v_scratch", [CT, P, TT * P], F32).ap()
        vnat_dram = nc.dram_tensor("attn_v_scratch", [T, 4 * P], F32).ap()
        o_dram = nc.dram_tensor("attn_out_scratch", [2, T, ROW], F32).ap()
        tab_dram = nc.dram_tensor("bias_rows_scratch", [24, TABW], F32).ap()
        skew_dram = nc.dram_tensor("bias_skew_scratch", [24, P * TABW], F32).ap()

        ident_in, par_in = sem("ident_in"), sem("par_in")
        ws_in, bs_in, tab_in = sem("ws_in"), sem("bs_in"), sem("tab_in")
        x_in = [sem(f"x_in{t}") for t in range(TT)]
        pool_step = sem("pool_step")
        consts_ready = sem("consts_ready")
        tab_stored, skew_stored = sem("tab_stored"), sem("skew_stored")
        ws_masked = sem("ws_masked")
        col_in = [sem(f"col_in{s}") for s in range(2)]
        wide_in = [sem(f"wide_in{s}") for s in range(2)]
        col_hi_done, col_lo_done = sem("col_hi_done"), sem("col_lo_done")
        wide_hi_done, wide_lo_done = sem("wide_hi_done"), sem("wide_lo_done")
        up_done, down_done = sem("up_done"), sem("down_done")
        up_free = [sem(f"up_free{b}") for b in range(2)]
        down_free = [sem(f"down_free{b}") for b in range(2)]
        xt_hi_done, res_scaled = sem("xt_hi_done"), sem("res_scaled")
        v_counted = sem("v_counted")
        v_stored = [sem(f"v_stored{k}") for k in range(4)]
        v_mean, v_scale, v_norm = sem("v_mean"), sem("v_scale"), sem("v_norm")
        v_loaded = [sem(f"v_loaded{s}") for s in range(2)]
        tap0_done, tap1_done, gate_act = sem("tap0_done"), sem("tap1_done"), sem("gate_act")
        y_done, hid_hi_done, hid_ready = sem("y_done"), sem("hid_hi_done"), sem("hid_ready")
        half_step = sem("half_step")
        gb_in = sem("gb_in")
        ln_squares, ln_mean, ln_scale = sem("ln_squares"), sem("ln_mean"), sem("ln_scale")
        ln_step, xn_done = sem("ln_step"), sem("xn_done")
        ln_act, xn_late = sem("ln_act"), sem("xn_late")
        out_stored = sem("out_stored")
        attn_v_stored = sem("attn_v_stored")
        logits_a, exp_done, turned, prob_t_ready = sem("logits_a"), sem("exp_done"), sem("turned"), sem("prob_t_ready")
        vp_in = [sem(f"vp_in{g}") for g in range(3)]
        bias_in = [sem(f"bias_in{g}") for g in range(3)]
        bias_clear = sem("bias_clear")
        nat_stored = [None, sem("nat_stored1"), sem("nat_stored2")]
        nat_in = [None, sem("nat_in1"), sem("nat_in2")]
        mix_step, mix_delta, mix_exp = sem("mix_step"), sem("mix_delta"), sem("mix_exp")
        o_done, o_hi_done = sem("o_done"), sem("o_hi_done")

        class Base:
            def __init__(self, col, wide, in0, up, in1=0, down=0, hid=0, tap=0):
                self.col, self.wide, self.in0, self.in1 = col, wide, in0, in1
                self.up, self.down, self.hid, self.tap = up, down, hid, tap

        SET_UP = 0
        X_DOWN = TT
        V1 = Base(col=0, wide=0, in0=0, in1=0, up=SET_UP + 6)
        G1 = Base(col=8, wide=8, in0=4, in1=4, up=V1.up + 16, down=X_DOWN + TT, hid=0)
        LN_DOWN = [G1.down + TT * SG]
        F1 = Base(col=G1.col + 2 * SG, wide=G1.wide + 2 * SG, in0=G1.in0 + SG, in1=G1.in1 + SG, up=G1.up + 4 * SG,
                  down=LN_DOWN[0] + TT, hid=2 * SG, tap=0)
        LN_DOWN.append(F1.down + TT * FI)
        V2 = Base(col=F1.col + 4 * FI, wide=F1.wide + 2 * FI, in0=F1.in0 + FI, in1=F1.in1 + FI, up=F1.up + 4 * FI,
                  down=LN_DOWN[1] + TT)
        PAIR_UP, PAIR_DOWN = 30, 24 + TT
        AT = Base(col=V2.col + 2, wide=V2.wide + 2, in0=V2.in0 + 1, up=V2.up + 4, down=V2.down)
        LN_DOWN.append(AT.down + NPAIR * PAIR_DOWN)
        F2 = Base(col=AT.col + 4 * NPAIR, wide=AT.wide + NPAIR, in0=AT.in0 + NPAIR, in1=V2.in1 + 1,
                  up=AT.up + NPAIR * PAIR_UP, down=LN_DOWN[2] + TT, hid=F1.hid + 2 * FI, tap=4 * FI)
        LN_DOWN.append(F2.down + TT * FI)
        Q2_UP, Q0_UP, NEXT_UP = 2, 11, 28
        ORDER = (2, 1, 0)
        STEP_DOWN = {2: 0, 1: 8, 0: 16}

        def step_up(k):
            return 3 + k if k < 8 else 4 + k

        def freed(base, j, more=0):
            return base // 2 + j + 2 + more

        def wait_apart(eng, *waits):
            waits = [(to, eng.to_reg(value)) for to, value in waits]
            eng.wait_ge(consts_ready, 2)
            for to, value in waits:
                eng.wait_ge(to, value)

        def wait_normalized(eng, n, t):
            if t < EARLY:
                eng.wait_ge(xn_done, EARLY * n + t + 1)
            else:
                eng.wait_ge(xn_late, (TT - EARLY) * n + t - EARLY + 1)

        def wait_turned(eng, n, tiles=TT):
            at = X_DOWN if n == 0 else LN_DOWN[n - 1]
            for b in range(2):
                eng.wait_ge(down_free[b], freed(at, (tiles - 1 - b) // 2))

        def col_piece(w, at, i, step):
            n = w.shape[1] // (step * P)
            v = w.rearrange("(k p) (i s n) -> i s p k n", p=P, s=step, n=P)
            return v[ds(i, 1), at].rearrange("a p k n -> (a p) k n")

        def row_piece(w, at, i, step):
            v = w.rearrange("(i s p) n -> i s p n", s=step, p=P)
            return v[ds(i, 1), at].rearrange("a p n -> (a p) n")

        w_u, w_v = a_w_in[0][:, 0:W_SGU], a_w_in[0][:, W_SGU:2 * W_SGU]
        w_out, w_q, w_o = a_w_out[0], b_w_q[0], b_w_o[0]
        w_k, w_kv = kv_w[:, 0:4 * P], kv_w[:, 4 * P:8 * P]
        wide_k_hi = wide_hi[:].rearrange("p s (k n) -> p s k n", n=P)
        wide_k_lo = wide_lo[:].rearrange("p s (k n) -> p s k n", n=P)
        conv = par[:, 0:4, :].rearrange("p (l b) (j g i s) -> p l b j g i s", l=2, j=2, g=2, s=2)

        def tap(l, k, q, i):
            return conv[:, l, k // 2, k % 2, q // 2, ds(i, 1), q % 2]

        def steps():
            out = []
            for g in ORDER:
                for k in range(8):
                    first = (k == 0, k % 2 == 0, True)[g]
                    out.append((g, k, [k] if first else [k - 1, k], P if first else 2 * P))
            return out

        def tokens(a, g, t, n):
            if g == 0:
                return a[:, (t + 1 - n) * P:(t + 1) * P]
            if g == 1:
                v = a.rearrange("p (s r) -> p r s", r=4)[:, t // 2]
                return v if n == 2 else v[:, (t % 2) * P:(t % 2 + 1) * P]
            return a.rearrange("p (s t h) -> p t h s", t=8, h=2)[:, t]

        H_PRODUCT, H_TAP0, H_TAP1, H_TAP2, H_GATE, H_HI, H_LO = 1, 2, 3, 4, 5, 6, 7

        block = ctx.enter_context(nc.Block())

        @block.sync
        def _(sp):
            def col_load(B, j, s, src):
                sp.wait_ge(col_lo_done, B.col + 2 * j + s + 1)
                sp.dma_start(raw_col[:, s], src).then_inc(col_in[s], DMA)

            def wide_load(B, j, s, src):
                sp.wait_ge(wide_lo_done, B.wide + 2 * j + s + 1)
                sp.dma_start(raw_wide[:, s], src).then_inc(wide_in[s], DMA)

            def wide_col_load(B, j, s, src):
                sp.wait_ge(wide_lo_done, B.wide + 2 * j + s + 1)
                sp.dma_start(raw_wide[:, s].rearrange("p (k n) -> p k n", n=P), src).then_inc(wide_in[s], DMA)

            sp.dma_start(ident[:], identity).then_inc(ident_in, DMA)
            for t in range(TT):
                sp.dma_start(res[:, t], x[0, t * P:(t + 1) * P]).then_inc(x_in[t], DMA)

            def v_loads(i):
                for k in range(2):
                    col_load(V1, i, k, col_piece(w_v, k, i, 4))
                for k in range(2):
                    wide_col_load(V1, i, k, col_piece(w_v, 2 + k, i, 4))

            with sp.Fori(0, 1) as i:
                v_loads(i)
            rows = tmp[2]
            for l in range(2):
                for k in range(4):
                    src = ffn_conv_w[l, k:k + 1] if k < 3 else ffn_conv_b[l:l + 1]
                    sp.dma_start(rows[44 * (k % 2):44 * (k % 2) + 44, (2 * l + k // 2) * P:(2 * l + k // 2 + 1) * P],
                                 src.rearrange("a (r n) -> (a r) n", n=P)).then_inc(par_in, DMA)
            for k, src in enumerate((a_ln_g, a_ln_b)):
                sp.dma_start(rows[CT * k:CT * (k + 1), 4 * P:5 * P],
                             src.rearrange("a (r n) -> (a r) n", n=P)).then_inc(par_in, DMA)
            sp.wait_ge(consts_ready, 1)
            sp.dma_start(table[0:32, :], rel_table).then_inc(tab_in, DMA)
            sp.dma_start(pick[0:33, :], bucket_pick).then_inc(tab_in, DMA)
            sp.dma_start(ws_t.rearrange("p (g s) -> p g s", g=SG), a_w_s[0].rearrange("g t s -> t g s")).then_inc(ws_in, DMA)
            sp.dma_start(bs_rows, a_b_s.rearrange("a g t -> a (g t)").to_broadcast([P, SG * P])).then_inc(bs_in, DMA)
            with sp.Fori(1, 4) as i:
                v_loads(i)
            with sp.Fori(0, SG) as i:
                for s in range(2):
                    col_load(G1, i, s, col_piece(w_u, s, i, 2))
                for k in range(2):
                    wide_load(G1, i, k, row_piece(w_out, k, i, 2))

            def ffn_loads(l, B):
                wu, wd = ffn_w_up[l], ffn_w_down[l]
                with sp.Fori(0, FI) as i:
                    for q in range(4):
                        half = wu[:, (q // 2) * D_FF:(q // 2 + 1) * D_FF]
                        col_load(B, 2 * i + q // 2, q % 2, col_piece(half, q % 2, i, 2))
                        if q % 2:
                            if l and q == 1:
                                sp.wait_ge(wide_lo_done, B.wide + 2)
                            if l and q == 3:
                                sp.wait_ge(o_done, NPAIR)
                            wide_load(B, i, q // 2, row_piece(wd, q // 2, i, 2))

            ffn_loads(0, F1)
            with sp.Fori(0, 1) as i:
                for k in range(2):
                    col_load(V2, i, k, col_piece(w_kv, k, i, 4))
                for k in range(2):
                    wide_col_load(V2, i, k, col_piece(w_kv, 2 + k, i, 4))
            with sp.Fori(0, NPAIR) as i:
                for q, src in enumerate((w_k, w_q[:, 4 * P:8 * P], w_q[:, 8 * P:12 * P], w_q[:, 0:4 * P])):
                    col_load(AT, 2 * i + q // 2, q % 2, col_piece(src, 0, i, 1))
                sp.wait_ge(wide_lo_done, AT.wide + i + 2)
                sp.dma_start(raw_wide[:, 0], row_piece(w_o, 0, i, 1)).then_inc(wide_in[0], DMA)
            ffn_loads(1, F2)
            for t in range(TT):
                wait_normalized(sp, 3, t)
                sp.dma_start(out[0, t * P:(t + 1) * P], xn[t]).then_inc(out_stored, DMA)
            sp.wait_ge(out_stored, DMA * TT)

        @block.gpsimd
        def _(pool):
            nc.gpsimd.memset(table[0:33, :], BIG).then_inc(consts_ready, ONE)
            nc.gpsimd.memset(ones, 1.0).then_inc(consts_ready, ONE)
            nc.gpsimd.memset(v_half, -0.5).then_inc(pool_step, ONE)
            pool.wait_ge(ws_in, DMA)
            wv = ws_t.rearrange("p (g s) -> p g s", g=SG)
            nc.gpsimd.affine_select(out=wv, in_=wv, compare_op=ALU.is_ge, fill=0.0, base=0,
                                    pattern=[[0, SG], [-1, P]], channel_multiplier=1).then_inc(ws_masked, ONE)
            for b in range(2):
                pool.wait_ge(up_free[b], freed(SET_UP, 1))
            for g in range(3):
                pool.dma_start(tab_dram[8 * g:8 * g + 8], tab_rows[0:8, g * TABW:(g + 1) * TABW]).then_inc(tab_stored, DMA)
            pool.wait_ge(tab_stored, 3 * DMA)
            for g in range(3):
                src = bass.AP(tensor=tab_dram.tensor, offset=8 * g * TABW, ap=[[TABW, 8], [0, P], [1, TABW]])
                pool.dma_start(skew_dram[8 * g:8 * g + 8].rearrange("h (p w) -> h p w", w=TABW), src).then_inc(skew_stored, DMA)
            vd = v_dram.rearrange("(i u c) p (q t n) -> i u c q p t n", u=2, c=2, q=2, t=4)
            with pool.Fori(0, 4) as i:
                for k in range(4):
                    u, q = k // 2, k % 2
                    wait_apart(pool, (up_free[q], freed(V1.up, u) + 2 * i))
                    for c in range(2):
                        pool.dma_start(vd[ds(i, 1), u, c, q].rearrange("a p t n -> (a p) t n"),
                                       tmp[k].rearrange("p (t c n) -> p t c n", t=4, c=2)[:, :, c, :]
                                       ).then_inc(v_stored[k], DMA)
            pool.wait_ge(v_mean, TT)
            nc.gpsimd.tensor_scalar(v_rstd, v_mv[:, :, 1], EPS, None, ALU.add).then_inc(pool_step, ONE)
            pool.wait_ge(pool_step, 2)
            nc.gpsimd.tensor_tensor(v_rstd, v_rstd, v_half, ALU.pow).then_inc(v_scale, ONE)
            for k in range(4):
                pool.wait_ge(v_stored[k], 8 * DMA)
            vl = v_dram.rearrange("(i s) p n -> i s p n", s=2)
            pool.wait_ge(up_free[1], freed(SET_UP, 2))
            with pool.Fori(0, SG) as i:
                for s in range(2):
                    wait_apart(pool, (up_done, G1.up + 4 * i - 2 + 2 * s))
                    pool.dma_start(v_in[s], vl[ds(i, 1), s].rearrange("a p n -> (a p) n")).then_inc(v_loaded[s], DMA)

            def add_bias(n, t):
                if t == 0:
                    pool.wait_ge(gb_in, 2 * DMA * (n + 1))
                pool.wait_ge(ln_act, EARLY * n + t + 1)
                nc.gpsimd.tensor_tensor(xn[t], xn[t], gb[:, D:2 * D], ALU.add).then_inc(xn_done, ONE)

            def norm_constants(n):
                for k, src in enumerate((ln_g, ln_b)):
                    pool.dma_start(gb[:, k * D:(k + 1) * D],
                                   src[n // 2, n % 2:n % 2 + 1].to_broadcast([P, D])).then_inc(gb_in, DMA)
                nc.gpsimd.memset(v_half, -0.5).then_inc(pool_step, ONE)
                pool.wait_ge(pool_step, 3 + (TT + 1) * n)
                lag = TT if n == 2 else 2
                for t in range(TT):
                    pool.wait_ge(ln_squares, TT * n + t + 1)
                    nc.gpsimd.tensor_scalar(ln_rstd[:, t:t + 1], ln_mv[:, t, 1:2], 1.0 / D, EPS, ALU.mult, ALU.add
                                            ).then_inc(pool_step, ONE)
                    pool.wait_ge(pool_step, 3 + (TT + 1) * n + t + 1)
                    nc.gpsimd.tensor_tensor(ln_rstd[:, t:t + 1], ln_rstd[:, t:t + 1], v_half[:, 0:1], ALU.pow
                                            ).then_inc(ln_scale, ONE)
                    if lag <= t < EARLY + lag:
                        add_bias(n, t - lag)
                for t in range(min(TT - lag, EARLY), EARLY):
                    add_bias(n, t)

            norm_constants(0)
            wait_turned(pool, 1)
            norm_constants(1)
            pool.wait_ge(res_scaled, 3 * TT)
            nc.gpsimd.memset(bias[2], BIG).then_inc(bias_clear, ONE)
            for k in range(4):
                pool.wait_ge(up_free[k % 2], freed(V2.up, k // 2))
                u, q = k // 2, k % 2
                dst = vnat_dram.rearrange("(q t p) (u n) -> q u p t n", q=2, t=4, u=2)[q, u]
                pool.dma_start(dst, tmp[k].rearrange("p (t n) -> p t n", t=4)).then_inc(attn_v_stored, DMA)
            pool.wait_ge(attn_v_stored, 4 * DMA)
            pool.wait_ge(bias_clear, 1)
            pool.wait_ge(skew_stored, 3 * DMA)
            v_tok = [vnat_dram.rearrange("(t p) (i c) -> i p t c", p=P, i=NPAIR),
                     vnat_dram.rearrange("(n p r) (i c) -> i r p n c", n=2, r=4, i=NPAIR),
                     vnat_dram.rearrange("(s t h) (i c) -> i h s t c", s=HD, h=2, i=NPAIR)]
            o_tok = [None, o_dram[0].rearrange("(n p r) c -> r p n c", n=2, r=4),
                     o_dram[1].rearrange("(s t h) c -> h s t c", s=HD, h=2)]

            def skewed(g, hh, at, n, w, i):
                sk = skew_dram[8 * g:8 * g + 8].rearrange("(i h) n -> i h n", h=2)[:, hh]
                v = sk[:, at:at + n * (TABW - 1)].rearrange("i (p w) -> i p w", w=TABW - 1)[:, :, 0:w]
                return v[ds(i, 1)].rearrange("a p w -> (a p) w")

            with pool.Fori(0, NPAIR) as i:
                d = AT.down + PAIR_DOWN * i
                wait_apart(pool, (down_done, d - TT))
                for h in range(2):
                    pool.dma_start(v_perm[0][h * HD:(h + 1) * HD],
                                   v_tok[2][ds(i, 1), h].rearrange("a s t c -> (a s) t c")).then_inc(vp_in[2], DMA)
                for hh in range(2):
                    for h in range(2):
                        pool.dma_start(bias[2][h * HD:(h + 1) * HD, hh, h * HD:(h + 1) * HD],
                                       skewed(2, hh, 255, HD, HD, i)).then_inc(bias_in[2], DMA)
                for hh in range(2):
                    pool.dma_start(bias[1][:, hh], skewed(1, hh, 127, P, 256, i)).then_inc(bias_in[1], DMA)
                for r in range(4):
                    pool.dma_start(v_perm[1][:, 2 * r:2 * r + 2],
                                   v_tok[1][ds(i, 1), r].rearrange("a p n c -> (a p) n c")).then_inc(vp_in[1], DMA)
                for hh in range(2):
                    pool.dma_start(bias[0][:, hh], skewed(0, hh, 127, P, 256, i)).then_inc(bias_in[0], DMA)
                wait_apart(pool, (down_done, d + 8))
                pool.dma_start(v_perm[0], v_tok[0][ds(i, 1)].rearrange("a p t c -> (a p) t c")).then_inc(vp_in[0], DMA)
                for g in (2, 1):
                    wait_apart(pool, *[(down_free[b], freed(AT.down + STEP_DOWN[g], 3) + PAIR_DOWN // 2 * i) for b in range(2)])
                    if g == 2:
                        for h in range(2):
                            pool.dma_start(o_tok[2][h], nat[2][h * HD:(h + 1) * HD]).then_inc(nat_stored[2], DMA)
                    else:
                        for r in range(4):
                            pool.dma_start(o_tok[1][r], nat[1][:, 2 * r:2 * r + 2]).then_inc(nat_stored[1], DMA)
                    stores = 2 if g == 2 else 4
                    wait_apart(pool, (nat_stored[g], stores * DMA * i + stores * DMA))
                    pool.dma_start(nat[g], o_dram[g - 1].rearrange("(t p) c -> p t c", p=P)).then_inc(nat_in[g], DMA)
            pool.wait_ge(o_done, NPAIR)
            norm_constants(2)
            wait_turned(pool, 3)
            norm_constants(3)

        @block.scalar
        def _(act):
            def hi_col(B, j, s, fills):
                act.wait_ge(col_in[s], DMA * (B.col // 2 + 1) + DMA * j)
                act.wait_ge(up_done, fills)
                nc.scalar.activation(col_hi[:, s], raw_col[:, s], ACT.Copy).then_inc(col_hi_done, ONE)

            def hi_wide(came, j, k, downs=None, fills=None):
                act.wait_ge(wide_in[k], DMA * (came + 1) + DMA * j)
                if downs is not None:
                    act.wait_ge(down_done, downs)
                if fills is not None:
                    act.wait_ge(up_done, fills)
                nc.scalar.activation(wide_hi[:, k], raw_wide[:, k], ACT.Copy).then_inc(wide_hi_done, ONE)

            for t in range(TT):
                act.wait_ge(down_done, X_DOWN + t + 1)
                nc.scalar.activation(xt_hi[:, :, t * P:(t + 1) * P], down[t % 2][:].rearrange("p (k t) -> p k t", k=KT),
                                     ACT.Copy).then_inc(xt_hi_done, ONE)
                nc.scalar.mul(res[:, t], res[:, t], ALPHA).then_inc(res_scaled, ONE)
            for s in range(2):
                hi_col(V1, 0, s, 1)
            act.wait_ge(up_done, SET_UP + 1)
            nc.scalar.copy(par[:, 0:4], up[0][:, 0:4 * P].rearrange("p (b n) -> p b n", b=4)[:, :, 0:88]).then_inc(up_free[0], ONE)
            act.wait_ge(up_done, SET_UP + 2)
            nc.scalar.copy(par[:, 4, 0:32], up[1][:, 0:32]).then_inc(up_free[1], ONE)
            act.wait_ge(up_done, SET_UP + 3)
            nc.scalar.copy(tab_rows[0:8, 0:2 * TABW].rearrange("p (g n) -> p g n", g=2),
                           up[0][0:8].rearrange("p (g n) -> p g n", g=2)[:, :, 0:TABW]).then_inc(up_free[0], ONE)
            act.wait_ge(up_done, SET_UP + 4)
            nc.scalar.copy(tab_rows[0:8, 2 * TABW:], up[1][0:8, 0:TABW]).then_inc(up_free[1], ONE)
            act.wait_ge(up_done, SET_UP + 5)
            nc.scalar.copy(ws_t, up[0][:]).then_inc(up_free[0], ONE)

            def v_tiles(i, u, first):
                for q in range(2):
                    k = 2 * u + q
                    act.wait_ge(up_done, V1.up + 4 * i + k + 1)
                    act.wait_ge(v_counted, 4 * i + k + 1)
                    if not first:
                        act.wait_ge(v_stored[k], 2 * DMA * i)
                    nc.scalar.activation(tmp[k], up[q][:], ACT.Gelu).then_inc(up_free[q], ONE)

            for start, end in ((0, 1), (1, 4)):
                with act.Fori(start, end) as i:
                    for k in range(2):
                        hi_wide(V1.in0, i, k, fills=V1.up + 4 * i)
                    v_tiles(i, 0, start == 0)
                    for s in range(2):
                        hi_col(V1, i + 1, s, V1.up + 4 * i + 2)
                    v_tiles(i, 1, start == 0)

            def hid_hi_part(B, i, s):
                act.wait_ge(y_done, B.hid + 2 * i + s + 3)
                act.wait_ge(down_done, B.down + TT * i)
                nc.scalar.activation(hid_hi[:, s], tmp[2 + s], ACT.Copy).then_inc(hid_hi_done, ONE)

            for k in range(4):
                act.wait_ge(v_stored[k], 8 * DMA)
            with act.Fori(0, SG) as i:
                for s in range(2):
                    act.wait_ge(up_done, G1.up + 4 * i + 2 * s + 1)
                    act.wait_ge(y_done, G1.hid + 2 * i + s + 1)
                    nc.scalar.activation(tmp[s], up[0][:], ACT.Gelu).then_inc(up_free[0], ONE)
                    hi_col(G1, i + 1, s, G1.up + 4 * i + 2 * s + 1)
                    if s == 0:
                        for k in range(2):
                            hi_wide(G1.in0, i, k, downs=G1.down + TT * i)
                    hid_hi_part(G1, i, s)

            def deviate(n, t):
                act.wait_ge(ln_step, TT * n + t + 1)
                act.wait_ge(ln_scale, TT * n + t + 1)
                nc.scalar.activation(xn[t], xn[t], ACT.Copy, scale=ln_rstd[:, t:t + 1]).then_inc(ln_act, ONE)

            def square_sums(n):
                lag = TT if n == 2 else 2
                for t in range(TT):
                    act.wait_ge(ln_mean, TT * n + t + 1)
                    if n or t:
                        act.wait_ge(ln_squares, TT * n + t)
                    nc.scalar.activation(squares, res[:, t], ACT.Square, scale=-1.0, bias=ln_mv[:, t, 0:1],
                                         accum_out=ln_mv[:, t, 1:2]).then_inc(ln_squares, ONE)
                    if lag <= t < EARLY + lag:
                        deviate(n, t - lag)
                for t in range(min(TT - lag, EARLY), EARLY):
                    deviate(n, t)

            def ln_out(n):
                square_sums(n)
                for t in range(TT):
                    act.wait_ge(down_done, LN_DOWN[n] + t + 1)
                    nc.scalar.activation(xt_hi[:, :, t * P:(t + 1) * P], down[t % 2][:].rearrange("p (k t) -> p k t", k=KT),
                                         ACT.Copy).then_inc(xt_hi_done, ONE)
                    nc.scalar.mul(res[:, t], xn[t], ALPHA).then_inc(res_scaled, ONE)
                act.wait_ge(res_scaled, TT * (n + 2))

            def ffn(l, B):
                def first_tap(i, q):
                    act.wait_ge(up_done, B.up + 4 * i + q + 1)
                    if q < 2:
                        act.wait_ge(y_done, B.hid + 2 * i + q + 1)
                    else:
                        act.wait_ge(hid_ready, B.hid + 2 * i + q - 2 - 1)
                    nc.scalar.activation(tmp[q], up[q % 2][:], ACT.Identity, bias=tap(l, 3, q, i),
                                         scale=tap(l, 2, q, i)).then_inc(tap0_done, ONE)

                def first_half(i):
                    act.wait_ge(half_step, 7 * l + H_PRODUCT)
                    act.wait_ge(hid_ready, B.hid + 2 * i)
                    nc.scalar.activation(tmp[3][:, 0:HALF], up[1][:, 0:HALF], ACT.Identity, bias=tap(l, 3, 3, i),
                                         scale=tap(l, 2, 3, i)).then_inc(half_step, ONE)
                    act.wait_ge(half_step, 7 * l + H_GATE)
                    act.wait_ge(down_done, B.down + TT * i)
                    nc.scalar.activation(hid_hi[:, 1, 0:HALF], tmp[3][:, 0:HALF], ACT.Copy).then_inc(half_step, ONE)

                def last_half(i):
                    act.wait_ge(up_done, B.up + 4 * i + 4)
                    nc.scalar.activation(tmp[3][:, HALF:], up[1][:, HALF:], ACT.Identity, bias=tap(l, 3, 3, i),
                                         scale=tap(l, 2, 3, i)).then_inc(tap0_done, ONE)
                    act.wait_ge(y_done, B.hid + 2 * i + 4)
                    nc.scalar.activation(hid_hi[:, 1, HALF:], tmp[3][:, HALF:], ACT.Copy).then_inc(hid_hi_done, ONE)

                def chunk(i, split_next, last_chunk):
                    for q in range(4):
                        if last_chunk and q == 3:
                            first_half(i)
                            last_half(i)
                        if q < 2 or split_next:
                            hi_col(B, 2 * i + 1 + q // 2, q % 2, B.up + 4 * i + q + 1)
                        if last_chunk and q == 3:
                            continue
                        first_tap(i, q)
                        if q < 2:
                            act.wait_ge(up_free[q], freed(B.up, 2 * i))
                            nc.scalar.activation(tmp[q], tmp[q], ACT.Gelu).then_inc(gate_act, ONE)
                        else:
                            hid_hi_part(B, i, q - 2)
                        if q == 1:
                            for k in range(2):
                                hi_wide(B.in0 if k == 0 else B.in1, i, k, downs=B.down + TT * i)

                with act.Fori(0, FI - 1) as i:
                    chunk(i, True, False)
                with act.Fori(FI - 1, FI) as i:
                    chunk(i, l == 0, True)

            ln_out(0)
            ffn(0, F1)
            ln_out(1)
            for k in range(2):
                hi_wide(V2.in0 if k == 0 else V2.in1, 0, k, downs=V2.down)
            for k in range(4):
                act.wait_ge(up_done, V2.up + k + 1)
                nc.scalar.copy(tmp[k], up[k % 2][:]).then_inc(up_free[k % 2], ONE)
                if k == 1:
                    for s in range(2):
                        hi_col(AT, 0, s, V2.up + 2)
            act.wait_ge(attn_v_stored, 4 * DMA)
            q_scale = -HD ** -0.5
            act.wait_ge(up_done, AT.up + 1)
            nc.scalar.copy(k_t, up[0][:]).then_inc(up_free[0], ONE)
            with act.Fori(0, 1) as i:
                hi_col(AT, i + 1, 0, AT.up + 1)
            act.wait_ge(up_done, AT.up + 2)
            nc.scalar.mul(q_t[1], up[1][:], q_scale).then_inc(up_free[1], ONE)
            with act.Fori(0, 1) as i:
                hi_col(AT, i + 1, 1, AT.up + 2)

            def group2_queries(fills):
                act.wait_ge(up_done, fills)
                nc.scalar.mul(q_t[0].rearrange("p (t h s) -> p t h s", t=8, h=2),
                              up[0][:].rearrange("p (s t h) -> p t h s", t=8, h=2), q_scale).then_inc(up_free[0], ONE)

            def pair(i, last):
                m = AT.up + PAIR_UP * i
                m2 = PAIR_UP // 2 * i
                d = AT.down + PAIR_DOWN * i
                for k in range(24 + 3):
                    if k == 11:
                        hi_col(AT, 2 * i + 2, 0, m + Q2_UP + 1)
                    if k == 9:
                        act.wait_ge(wide_in[0], DMA * (AT.in0 + 1) + DMA * i)
                        act.wait_ge(down_done, d)
                        nc.scalar.activation(wide_hi[:, 0], raw_wide[:, 0], ACT.Copy).then_inc(wide_hi_done, ONE)
                    if k == 8:
                        act.wait_ge(up_done, m + Q0_UP + 1)
                        nc.scalar.mul(q_t[0], up[1][:], q_scale).then_inc(up_free[1], ONE)
                    if k == 13:
                        hi_col(AT, 2 * i + 2, 1, m + Q0_UP + 1)
                    if k < 24:
                        g, t, keys, w = steps()[k]
                        p = prob[k % 4]
                        f = step_up(k)
                        for h in range(2):
                            if h == 0:
                                act.wait_ge(logits_a, 24 * i + k + 1)
                            else:
                                act.wait_ge(up_free[f % 2], freed(AT.up + f - f % 2, 0) + m2)
                            e = nc.scalar.activation(p[:, h, 0:w], p[:, h, 0:w], ACT.Exp, scale=-1.0,
                                                     bias=nat[g][:, t, 2 * HD + h:2 * HD + h + 1],
                                                     accum_out=nat[g][:, t, 2 * HD + 2 + h:2 * HD + 3 + h])
                        e.then_inc(exp_done, ONE)
                    if k >= 3:
                        g, t, _, _ = steps()[k - 3]
                        b = (k - 3) % 2
                        act.wait_ge(down_done, d + k - 3 + 1)
                        nc.scalar.copy(nat[g][:, t, 0:2 * HD], down[b][:, HALF:HALF + 2 * HD]).then_inc(down_free[b], ONE)
                act.wait_ge(mix_delta, i + 1)
                nc.scalar.activation(mix[:, 16:64], mix[:, 16:64], ACT.Exp).then_inc(mix_exp, ONE)
                turned_up = NEXT_UP
                if not last:
                    act.wait_ge(up_done, m + NEXT_UP + 1)
                    nc.scalar.copy(k_t, up[0][:]).then_inc(up_free[0], ONE)
                    hi_col(AT, 2 * i + 3, 0, m + NEXT_UP + 1)
                    act.wait_ge(up_done, m + NEXT_UP + 2)
                    nc.scalar.mul(q_t[1], up[1][:], q_scale).then_inc(up_free[1], ONE)
                    turned_up += 2
                for b in range(2):
                    act.wait_ge(up_done, m + turned_up + b + 1)
                    act.wait_ge(down_done, d)
                    nc.scalar.activation(hid_hi[:, 0, b * HALF:(b + 1) * HALF], up[b][:, 0:HALF], ACT.Copy).then_inc(o_hi_done, ONE)
                if not last:
                    hi_col(AT, 2 * i + 3, 1, m + NEXT_UP + 2)
                    group2_queries(m + PAIR_UP + Q2_UP + 1)

            group2_queries(AT.up + Q2_UP + 1)
            with act.Fori(0, NPAIR - 1) as i:
                pair(i, False)
            with act.Fori(NPAIR - 1, NPAIR) as i:
                pair(i, True)
            ln_out(2)
            ffn(1, F2)
            square_sums(3)

        @block.vector
        def _(dve):
            dve.sem_inc(col_lo_done, 2)
            dve.sem_inc(wide_lo_done, 2)
            dve.sem_inc(v_counted, 4)
            dve.sem_inc(y_done, 2)

            def lo_col(B, j, s):
                dve.wait_ge(col_hi_done, B.col + 2 * j + s + 1)
                nc.vector.tensor_tensor(col_lo[:, s], raw_col[:, s], col_hi[:, s], ALU.subtract).then_inc(col_lo_done, ONE)

            def lo_wide(n, k):
                dve.wait_ge(wide_hi_done, n + 1)
                nc.vector.tensor_tensor(wide_lo[:, k], raw_wide[:, k], wide_hi[:, k], ALU.subtract).then_inc(wide_lo_done, ONE)

            def turned_lo(n, at, t):
                dve.wait_ge(xt_hi_done, TT * n + t + 1)
                tk = slice(t * P, (t + 1) * P)
                nc.vector.tensor_tensor(xt_lo[:, :, tk], down[t % 2][:].rearrange("p (k t) -> p k t", k=KT),
                                        xt_hi[:, :, tk], ALU.subtract).then_inc(down_free[t % 2], ONE)

            def add_down(at):
                for t in range(TT):
                    dve.wait_ge(down_done, at + t + 1)
                    nc.vector.tensor_tensor(res[:, t], down[t % 2][:], res[:, t], ALU.add).then_inc(down_free[t % 2], ONE)

            for t in range(TT):
                turned_lo(0, X_DOWN, t)
            dve.wait_ge(res_scaled, TT)
            for s in range(2):
                lo_col(V1, 0, s)
            dve.wait_ge(bs_in, DMA)
            dve.wait_ge(tab_stored, 3 * DMA)
            dve.wait_ge(up_free[1], freed(SET_UP, 0))
            dve.wait_ge(up_done, SET_UP + 6)
            for c in range(CT):
                g = c // 2
                last = nc.vector.scalar_tensor_tensor(out=bias_ts[:, c], in0=up[1][:, g * P:(g + 1) * P],
                                                      scalar=par[:, 4, CT + c:CT + c + 1], in1=bs_rows[:, g * P:(g + 1) * P],
                                                      op0=ALU.mult, op1=ALU.add)
            last.then_inc(up_free[1], ONE)

            def count_v(i, u):
                for q in range(2):
                    dve.wait_ge(up_free[q], freed(V1.up, u) + 2 * i)
                    for t in range(4):
                        last = nc.vector.bn_stats(v_stats.rearrange("p t (i u) x -> p t i u x", u=2)[:, 4 * q + t, ds(i, 1), u]
                                                  .rearrange("p a x -> p (a x)"),
                                                  tmp[2 * u + q][:, t * 2 * P:(t + 1) * 2 * P])
                    last.then_inc(v_counted, ONE)

            with dve.Fori(0, 4) as i:
                for k in range(2):
                    lo_wide(V1.wide + 2 * i + k, k)
                count_v(i, 0)
                for s in range(2):
                    lo_col(V1, i + 1, s)
                count_v(i, 1)
            dve.wait_ge(v_counted, 4 + 16)
            for t in range(TT):
                nc.vector.bn_aggr(v_mv[:, t], v_stats[:, t].rearrange("p j x -> p (j x)")).then_inc(v_mean, ONE)

            def hid_lo_part(B, i, s):
                dve.wait_ge(hid_hi_done, B.hid + 2 * i + s + 1)
                nc.vector.tensor_tensor(hid_lo[:, s], tmp[2 + s], hid_hi[:, s], ALU.subtract).then_inc(hid_ready, ONE)

            def normalize_v(i, s):
                dve.wait_ge(v_loaded[s], DMA * i + DMA)
                for t in range(TT):
                    last = nc.vector.tensor_scalar(v_in[s][:, t * P:(t + 1) * P], v_in[s][:, t * P:(t + 1) * P],
                                                   v_mv[:, t, 0:1], v_rstd[:, t:t + 1], ALU.subtract, ALU.mult)
                last.then_inc(v_norm, ONE)

            def layer_norm(n, down_at, turn):
                def add_and_count(t):
                    b = t % 2
                    dve.wait_ge(down_done, down_at + t + 1)
                    nc.vector.tensor_tensor_reduce(res[:, t], down[b][:], res[:, t], 1.0, 0.0, ALU.add, ALU.add,
                                                   ln_sum[:, t:t + 1]).then_inc(down_free[b], ONE)
                    dve.wait_ge(down_free[b], freed(down_at, t // 2))
                    nc.vector.tensor_scalar(ln_mv[:, t, 0:1], ln_sum[:, t:t + 1], 1.0 / D, None, ALU.mult).then_inc(ln_mean, ONE)

                def normalize(u):
                    if u == 0:
                        dve.wait_ge(gb_in, 2 * DMA * (n + 1))
                    dve.wait_ge(ln_mean, TT * n + u + 1)
                    nc.vector.scalar_tensor_tensor(out=xn[u], in0=res[:, u], scalar=ln_mv[:, u, 0:1], in1=gb[:, 0:D],
                                                   op0=ALU.subtract, op1=ALU.mult).then_inc(ln_step, ONE)

                lag = TT if n == 2 else 1
                for t in range(TT):
                    add_and_count(t)
                    if t >= lag:
                        normalize(t - lag)
                for t in range(TT - lag, TT):
                    normalize(t)

                def finish(u):
                    dve.wait_ge(ln_step, TT * n + u + 1)
                    dve.wait_ge(ln_scale, TT * n + u + 1)
                    nc.vector.scalar_tensor_tensor(out=xn[u], in0=xn[u], scalar=ln_rstd[:, u:u + 1], in1=gb[:, D:2 * D],
                                                   op0=ALU.mult, op1=ALU.add).then_inc(xn_late, ONE)

                if not turn:
                    for t in range(EARLY, TT):
                        finish(t)
                else:
                    for t in range(TT):
                        turned_lo(n + 1, LN_DOWN[n], t)
                        if t < TT - EARLY:
                            finish(t + EARLY)
                    dve.wait_ge(res_scaled, TT * (n + 2))

            def gated(i, last_group):
                for s in range(2):
                    lo_col(G1, i + 1, s)
                    if s == 0:
                        for k in range(2):
                            lo_wide(G1.wide + 2 * i + k, k)
                    dve.wait_ge(up_done, G1.up + 4 * i + 2 * s + 2)
                    gain = par[:, 4, 0:CT].rearrange("p (i s) -> p i s", s=2)[:, ds(i, 1), s]
                    term = bias_ts.rearrange("p (i s) t -> p i s t", s=2)[:, ds(i, 1), s].to_broadcast([P, TT, P])
                    nc.vector.scalar_tensor_tensor(out=tmp[2 + s].rearrange("p (t n) -> p t n", t=TT),
                                                   in0=up[1][:].rearrange("p (t n) -> p t n", t=TT), scalar=gain,
                                                   in1=term, op0=ALU.mult, op1=ALU.add).then_inc(up_free[1], ONE)
                    dve.wait_ge(up_free[1], freed(G1.up, s) + 2 * i)
                    dve.wait_ge(up_free[0], freed(G1.up, s) + 2 * i)
                    nc.vector.tensor_tensor(tmp[2 + s], tmp[2 + s], tmp[s], ALU.mult).then_inc(y_done, ONE)
                    hid_lo_part(G1, i, s)
                    if not last_group:
                        normalize_v(i + 1, s)
                if not last_group:
                    add_down(G1.down + TT * i)

            dve.wait_ge(v_scale, 1)
            dve.wait_ge(v_mean, TT)
            for s in range(2):
                normalize_v(0, s)
            with dve.Fori(0, SG - 1) as i:
                gated(i, False)
            with dve.Fori(SG - 1, SG) as i:
                gated(i, True)
            layer_norm(0, LN_DOWN[0] - TT, True)

            def ffn(l, B):
                def other_taps(i, q):
                    dve.wait_ge(tap0_done, B.tap + 4 * i + q + 1)
                    b = q % 2
                    nc.vector.scalar_tensor_tensor(out=tmp[q][:, 1:T], in0=up[b][:, 0:T - 1], scalar=tap(l, 1, q, i),
                                                   in1=tmp[q][:, 1:T], op0=ALU.mult, op1=ALU.add).then_inc(tap1_done, ONE)
                    dve.wait_ge(tap1_done, B.tap + 4 * i + q + 1)
                    nc.vector.scalar_tensor_tensor(out=tmp[q][:, 2:T], in0=up[b][:, 0:T - 2], scalar=tap(l, 0, q, i),
                                                   in1=tmp[q][:, 2:T], op0=ALU.mult, op1=ALU.add).then_inc(up_free[b], ONE)

                def half(i, h):
                    def signal(ins, last_of):
                        ins.then_inc(last_of if h else half_step, ONE)

                    def wait(last_of, count, first_of):
                        if h:
                            dve.wait_ge(last_of, count)
                        else:
                            dve.wait_ge(half_step, 7 * l + first_of)

                    for back, tap_at, of, first_of in ((1, 1, tap0_done, H_TAP0), (2, 0, tap1_done, H_TAP1)):
                        wait(of, B.tap + 4 * i + 4, first_of)
                        at = HALF if h else back
                        to = slice(at, at + HALF if h else HALF)
                        signal(nc.vector.scalar_tensor_tensor(out=tmp[3][:, to], in0=up[1][:, to.start - back:to.stop - back],
                                                              scalar=tap(l, tap_at, 3, i), in1=tmp[3][:, to],
                                                              op0=ALU.mult, op1=ALU.add),
                               tap1_done if back == 1 else up_free[1])
                    hs = slice(h * HALF, (h + 1) * HALF)
                    wait(up_free[1], freed(B.up, 1) + 2 * i, H_TAP2)
                    dve.wait_ge(gate_act, B.tap // 2 + 2 * i + 2)
                    signal(nc.vector.tensor_tensor(tmp[3][:, hs], tmp[3][:, hs], tmp[1][:, hs], ALU.mult), y_done)
                    wait(hid_hi_done, B.hid + 2 * i + 2, H_HI)
                    signal(nc.vector.tensor_tensor(hid_lo[:, 1, hs], tmp[3][:, hs], hid_hi[:, 1, hs], ALU.subtract), hid_ready)

                def chunk(i, split_next, last_chunk):
                    for q in range(4):
                        if last_chunk and q == 3:
                            half(i, 0)
                            half(i, 1)
                        if q < 2 or split_next:
                            lo_col(B, 2 * i + 1 + q // 2, q % 2)
                        if last_chunk and q == 3:
                            continue
                        other_taps(i, q)
                        if q >= 2:
                            s = q - 2
                            dve.wait_ge(up_free[s], freed(B.up, 1) + 2 * i)
                            dve.wait_ge(gate_act, B.tap // 2 + 2 * i + s + 1)
                            nc.vector.tensor_tensor(tmp[q], tmp[q], tmp[s], ALU.mult).then_inc(y_done, ONE)
                            hid_lo_part(B, i, s)
                        if q == 1:
                            for k in range(2):
                                lo_wide(B.wide + 2 * i + k, k)

                with dve.Fori(0, FI - 1) as i:
                    chunk(i, True, False)
                    add_down(B.down + TT * i)
                with dve.Fori(FI - 1, FI) as i:
                    chunk(i, l == 0, True)

            ffn(0, F1)
            layer_norm(1, LN_DOWN[1] - TT, True)
            for k in range(2):
                lo_wide(V2.wide + k, k)
            for s in range(2):
                lo_col(AT, 0, s)
            dve.wait_ge(attn_v_stored, 4 * DMA)
            def mix_groups(i):
                MIX = 11
                count = [0]

                def link(ins):
                    ins.then_inc(mix_step, ONE)
                    count[0] += 1
                    dve.wait_ge(mix_step, MIX * i + count[0])

                for g in (1, 2):
                    dve.wait_ge(nat_in[g], DMA * i + DMA)
                for b in range(2):
                    dve.wait_ge(down_free[b], freed(AT.down + STEP_DOWN[0], 3) + PAIR_DOWN // 2 * i)

                def stat(g, at):
                    return nat[g][:, :, 2 * HD + at:2 * HD + at + 2]

                def small(n):
                    return mix[:, 16 * n:16 * n + 16].rearrange("p (t h) -> p t h", t=TT)

                tt = nc.vector.tensor_tensor
                link(tt(small(0), stat(0, 0), stat(1, 0), ALU.min))
                link(tt(small(0), small(0), stat(2, 0), ALU.min))
                for g in range(3):
                    last = tt(small(1 + g), small(0), stat(g, 0), ALU.subtract)
                last.then_inc(mix_delta, ONE)
                dve.wait_ge(mix_exp, i + 1)
                for g in range(3):
                    last = tt(small(4 + g), small(1 + g), stat(g, 2), ALU.mult)
                link(last)
                link(tt(small(4), small(4), small(5), ALU.add))
                link(tt(small(4), small(4), small(6), ALU.add))
                link(nc.vector.reciprocal(small(7), small(4)))
                for g in range(3):
                    last = tt(small(1 + g), small(1 + g), small(7), ALU.mult)
                link(last)
                for g in range(3):
                    v = nat[g][:, :, 0:2 * HD].rearrange("p t (h d) -> p t h d", h=2)
                    wb = small(1 + g).rearrange("p t (h o) -> p t h o", o=1).to_broadcast([P, TT, 2, HD])
                    link(tt(v, v, wb, ALU.mult))
                o = q_t[0].rearrange("p (t c) -> p t c", t=TT)
                link(tt(o, nat[0][:, :, 0:2 * HD], nat[1][:, :, 0:2 * HD], ALU.add))
                tt(o, o, nat[2][:, :, 0:2 * HD], ALU.add).then_inc(o_done, ONE)

            def pair(i, last):
                for k in range(24 + 2):
                    if k == 10:
                        lo_wide(AT.wide + i, 0)
                    if k == 12:
                        lo_col(AT, 2 * i + 2, 0)
                    if k == 14:
                        lo_col(AT, 2 * i + 2, 1)
                    if k < 24:
                        g, t, keys, w = steps()[k]
                        if t == 0:
                            dve.wait_ge(bias_in[g], (4 if g == 2 else 2) * DMA * (i + 1))
                        f = step_up(k)
                        wait_apart(dve, (up_done, AT.up + PAIR_UP * i + f + 1))
                        for h in range(2):
                            nc.vector.tensor_tensor_reduce(prob[k % 4][:, h, 0:w], up[f % 2][:, h * HALF:h * HALF + w],
                                                           bias[g][:, h, b_w[g] - w:b_w[g]], 1.0, 3e38, ALU.add, ALU.min,
                                                           nat[g][:, t, 2 * HD + h:2 * HD + h + 1]
                                                           ).then_inc(up_free[f % 2] if h else logits_a, ONE)
                    if k >= 2:
                        j = k - 2
                        w = steps()[j][3]
                        dve.wait_ge(turned, 24 * i + j + 1)
                        dve.wait_ge(down_done, AT.down + PAIR_DOWN * i + j - 1)
                        nc.vector.tensor_copy(prob_t[j % 2][:, :, 0:w],
                                              down[j % 2][:, 0:HALF].rearrange("p (h w) -> p h w", h=2)[:, :, 0:w]
                                              ).then_inc(prob_t_ready, ONE)
                mix_groups(i)
                if not last:
                    lo_col(AT, 2 * i + 3, 0)
                for b in range(2):
                    dve.wait_ge(o_hi_done, 2 * i + b + 1)
                    nc.vector.tensor_tensor(hid_lo[:, 0, b * HALF:(b + 1) * HALF], up[b][:, 0:HALF], hid_hi[:, 0, b * HALF:(b + 1) * HALF],
                       ALU.subtract).then_inc(up_free[b], ONE)
                if not last:
                    lo_col(AT, 2 * i + 3, 1)
                    add_down(AT.down + PAIR_DOWN * i + 24)

            with dve.Fori(0, 1) as i:
                for s in range(2):
                    lo_col(AT, i + 1, s)
            with dve.Fori(0, NPAIR - 1) as i:
                pair(i, False)
            with dve.Fori(NPAIR - 1, NPAIR) as i:
                pair(i, True)
            layer_norm(2, LN_DOWN[2] - TT, True)
            ffn(1, F2)
            layer_norm(3, LN_DOWN[3] - TT, False)

        @block.tensor
        def _(pe):
            for b in range(2):
                pe.sem_inc(up_free[b], 1)
                pe.sem_inc(down_free[b], X_DOWN // 2 + 1)
            pe.sem_inc(down_done, X_DOWN)

            def mm(o, a, b, start, stop, **kw):
                return nc.tensor.matmul(o, a, b, start=start, stop=stop, **kw)

            def split_mm(o, a, b, first, last):
                mm(o, a[0], b[0], first, False)
                mm(o, a[0], b[1], False, False)
                return mm(o, a[1], b[0], False, last)

            def up_free_for(at, j):
                pe.wait_ge(up_free[at % 2], at // 2 + 1 + j)

            def turn(at, t, tile):
                pe.wait_ge(down_free[t % 2], (at + t) // 2 + 1)
                for k in range(KT):
                    last = nc.tensor.transpose(down[t % 2][:, k * P:(k + 1) * P], tile[:, k * P:(k + 1) * P], ident[:])
                last.then_inc(down_done, ONE)

            def turn_xn(n, tiles):
                for t in tiles:
                    wait_normalized(pe, n, t)
                    turn(LN_DOWN[n], t, xn[t])

            def features(at, j, piece, s, halves=(0, 1), first=None):
                if halves[0] == 0:
                    pe.wait_ge(col_lo_done, piece + 3)
                    up_free_for(at, j)
                for h in halves:
                    for k in range(KT):
                        sl = slice(h * HALF, (h + 1) * HALF)
                        last = split_mm(up[at % 2][:, sl], (col_hi[:, s, k], col_lo[:, s, k]),
                                        (xt_hi[:, k, sl], xt_lo[:, k, sl]), k == 0, k == KT - 1)
                    if h == 0 and first is not None:
                        last.then_inc(first, ONE)
                if halves[-1] == 1:
                    last.then_inc(up_done, ONE)

            def down_part(t, ks, nk):
                for n in range(2):
                    sl = slice(n * HALF, (n + 1) * HALF)
                    tk = slice(t * P, (t + 1) * P)
                    for k in ks:
                        last = split_mm(down[t % 2][:, sl], (hid_hi[:, k, tk], hid_lo[:, k, tk]),
                                        (wide_hi[:, k, sl], wide_lo[:, k, sl]), k == 0, k == nk - 1)
                return last

            def down_unit(at, j, nk, late=None, start=0):
                for t in range(start, TT):
                    if late is not None and t == TT // 2:
                        pe.wait_ge(*late)
                    pe.wait_ge(down_free[t % 2], at // 2 + t // 2 + 1 + j)
                    down_part(t, range(nk), nk).then_inc(down_done, ONE)

            def v_half(at, j, q, hi, lo):
                up_free_for(at + q, j)
                for t in range(4):
                    tk = slice((4 * q + t) * P, (4 * q + t + 1) * P)
                    o = up[q][:, t * 2 * P:(t + 1) * 2 * P].rearrange("p (s n) -> p s n", s=2)
                    for k in range(KT):
                        last = split_mm(o, (xt_hi[:, k, tk], xt_lo[:, k, tk]), (hi[:, :, k], lo[:, :, k]),
                                        k == 0, k == KT - 1)
                last.then_inc(up_done, ONE)

            pe.wait_ge(ident_in, DMA)
            for t in range(TT):
                pe.wait_ge(x_in[t], DMA)
                turn(X_DOWN, t, res[:, t])
            pe.wait_ge(par_in, 10 * DMA)
            up_free_for(SET_UP, 0)
            for blk in range(4):
                last = nc.tensor.transpose(up[0][:, blk * P:blk * P + 88], tmp[2][0:88, blk * P:(blk + 1) * P], ident[0:88, 0:88])
            last.then_inc(up_done, ONE)
            up_free_for(SET_UP + 1, 0)
            nc.tensor.transpose(up[1][:, 0:32], tmp[2][0:32, 4 * P:5 * P], ident[0:32, 0:32]).then_inc(up_done, ONE)
            pe.wait_ge(tab_in, 2 * DMA)
            pe.wait_ge(consts_ready, 2)
            up_free_for(SET_UP + 2, 0)
            for g in range(2):
                last = mm(up[0][0:8, g * HALF:g * HALF + TABW], table[0:33, 8 * g:8 * g + 8],
                          pick[0:33, g * TABW:(g + 1) * TABW], True, True)
            last.then_inc(up_done, ONE)
            up_free_for(SET_UP + 3, 0)
            mm(up[1][0:8, 0:TABW], table[0:33, 16:24], pick[0:33, 2 * TABW:3 * TABW], True, True).then_inc(up_done, ONE)
            pe.wait_ge(ws_masked, 1)
            up_free_for(SET_UP + 4, 0)
            for g in range(SG):
                last = nc.tensor.transpose(up[0][:, g * P:(g + 1) * P], ws_t[:, g * P:(g + 1) * P], ident[:])
            last.then_inc(up_done, ONE)
            pe.wait_ge(up_free[0], freed(SET_UP, 2))
            up_free_for(SET_UP + 5, 0)
            for h in range(2):
                last = mm(up[1][:, h * HALF:(h + 1) * HALF], ones, ws_t[:, h * HALF:(h + 1) * HALF], True, True)
            last.then_inc(up_done, ONE)

            wait_turned(pe, 0)
            with pe.Fori(0, 4) as i:
                pe.wait_ge(col_lo_done, V1.col + 2 * i + 4)
                for q in range(2):
                    v_half(V1.up, 2 * i, q, col_hi, col_lo)
                pe.wait_ge(wide_lo_done, V1.wide + 2 * i + 4)
                for q in range(2):
                    v_half(V1.up + 2, 2 * i, q, wide_k_hi, wide_k_lo)

            def mixed(i, s):
                pe.wait_ge(v_norm, 2 * i + s + 1)
                up_free_for(G1.up + 2 * s + 1, 2 * i)
                for t in range(TT):
                    last = mm(up[1][:, t * P:(t + 1) * P], v_in[s][:, t * P:(t + 1) * P],
                              ws_t.rearrange("p (g t) -> p g t", g=SG)[:, ds(i, 1)].rearrange("p a t -> p (a t)"), True, True)
                last.then_inc(up_done, ONE)

            def gated(i, last_group):
                mixed(i, 0)
                features(G1.up + 2, 2 * i, G1.col + 2 * i + 1, 1)
                mixed(i, 1)
                if not last_group:
                    features(G1.up + 4, 2 * i, G1.col + 2 * i + 2, 0)
                pe.wait_ge(wide_lo_done, G1.wide + 2 * i + 4)
                if last_group:
                    pe.wait_ge(hid_ready, G1.hid + 2 * i + 1)
                    for t in range(2):
                        pe.wait_ge(down_free[t], G1.down // 2 + 1 + 4 * i)
                        down_part(t, [0], 2)
                pe.wait_ge(hid_ready, G1.hid + 2 * i + 2)
                if last_group:
                    for t in range(2):
                        down_part(t, [1], 2).then_inc(down_done, ONE)
                down_unit(G1.down, 4 * i, 2, start=2 if last_group else 0)

            features(G1.up, 0, G1.col, 0)
            with pe.Fori(0, SG - 1) as i:
                gated(i, False)
            with pe.Fori(SG - 1, SG) as i:
                gated(i, True)

            def ffn(B, n):
                def chunk(i, last_chunk):
                    features(B.up + 2, 2 * i, B.col + 4 * i + 2, 0)
                    features(B.up + 3, 2 * i, B.col + 4 * i + 3, 1, first=half_step if last_chunk else None)
                    if last_chunk:
                        pe.wait_ge(wide_lo_done, B.wide + 2 * i + 4)
                        pe.wait_ge(hid_ready, B.hid + 2 * i + 1)
                        pe.wait_ge(half_step, 7 * (n // 2) + H_LO)
                        down_unit(B.down, 4 * i, 2, late=(hid_ready, B.hid + 2 * i + 2))
                    else:
                        features(B.up + 4, 2 * i, B.col + 4 * i + 4, 0)
                        pe.wait_ge(hid_ready, B.hid + 2 * i + 2)
                        pe.wait_ge(wide_lo_done, B.wide + 2 * i + 4)
                        down_unit(B.down, 4 * i, 2)
                        features(B.up + 5, 2 * i, B.col + 4 * i + 5, 1)

                turn_xn(n, range(0, 5))
                wait_turned(pe, n + 1, 4)
                features(B.up, 0, B.col, 0, (0,))
                turn_xn(n, [5])
                features(B.up + 1, 0, B.col + 1, 1, (0,))
                turn_xn(n, [6, 7])
                wait_turned(pe, n + 1)
                features(B.up, 0, B.col, 0, (1,))
                features(B.up + 1, 0, B.col + 1, 1, (1,))
                with pe.Fori(0, FI - 1) as i:
                    chunk(i, False)
                with pe.Fori(FI - 1, FI) as i:
                    chunk(i, True)

            ffn(F1, 0)
            pe.wait_ge(col_lo_done, V2.col + 4)
            turn_xn(1, range(0, 5))
            wait_turned(pe, 2, 4)
            v_half(V2.up, 0, 0, col_hi, col_lo)
            turn_xn(1, range(5, TT))
            wait_turned(pe, 2)
            v_half(V2.up, 0, 1, col_hi, col_lo)
            pe.wait_ge(wide_lo_done, V2.wide + 4)
            for q in range(2):
                v_half(V2.up + 2, 0, q, wide_k_hi, wide_k_lo)

            def pair(i, last_pair):
                m2 = PAIR_UP // 2 * i
                d2 = PAIR_DOWN // 2 * i
                st = steps()
                pe.wait_ge(up_free[0], freed(AT.up + Q2_UP, 0) + m2)
                for k in range(24 + 3):
                    if k == 16:
                        pe.wait_ge(up_free[1], freed(AT.up + Q0_UP - 1, 0) + m2)
                    if k < 24:
                        g, t, keys, w = st[k]
                        q = q_t[1 if g == 1 else 0]
                        f = step_up(k)
                        up_free_for(AT.up + f, m2)
                        for h in range(2):
                            hp = slice(h * HD, (h + 1) * HD)
                            queries = q[hp, t * P:(t + 1) * P] if g == 2 else tokens(q[hp], g, t, 1)
                            last = mm(up[f % 2][:, h * HALF:h * HALF + w], queries,
                                      tokens(k_t[hp], g, t, len(keys)), True, True)
                        last.then_inc(up_done, ONE)
                    if 2 <= k < 26:
                        j = k - 2
                        pe.wait_ge(exp_done, 24 * i + j + 1)
                        if j < 2:
                            pe.wait_ge(down_free[j % 2], (AT.down + j) // 2 + 1 + d2)
                        for h in range(2):
                            for c in range(len(st[j][2])):
                                last = nc.tensor.transpose(down[j % 2][:, h * 2 * P + c * P:h * 2 * P + (c + 1) * P],
                                                           prob[j % 4][:, h, c * P:(c + 1) * P], ident[:])
                        last.then_inc(turned, ONE)
                    if k >= 3:
                        j = k - 3
                        g, t, keys, w = st[j]
                        if t == 0:
                            pe.wait_ge(vp_in[g], {2: 2, 1: 4, 0: 1}[g] * DMA * (i + 1))
                        pe.wait_ge(prob_t_ready, 24 * i + j + 1)
                        if j >= 2:
                            pe.wait_ge(down_free[j % 2], (AT.down + j) // 2 + 1 + d2)
                        v = v_perm[1 if g == 1 else 0]
                        for h in range(2):
                            for c, kt in enumerate(keys):
                                last = mm(down[j % 2][:, HALF + h * HD:HALF + (h + 1) * HD],
                                          prob_t[j % 2][:, h, c * P:(c + 1) * P], v[:, kt, h * HD:(h + 1) * HD],
                                          c == 0, c == len(keys) - 1)
                        last.then_inc(down_done, ONE)
                    if k == 7:
                        features(AT.up + Q0_UP, m2, AT.col + 4 * i + 3, 1)
                turned_up = NEXT_UP
                if not last_pair:
                    features(AT.up + NEXT_UP, m2, AT.col + 4 * i + 4, 0)
                    features(AT.up + NEXT_UP + 1, m2, AT.col + 4 * i + 5, 1)
                    turned_up += 2
                pe.wait_ge(o_done, i + 1)
                for b in range(2):
                    up_free_for(AT.up + turned_up + b, m2)
                    for t in range(4):
                        c = (4 * b + t) * P
                        last = nc.tensor.transpose(up[b][:, t * P:(t + 1) * P], q_t[0][:, c:c + P], ident[:])
                    last.then_inc(up_done, ONE)
                if not last_pair:
                    features(AT.up + PAIR_UP + Q2_UP, m2, AT.col + 4 * i + 6, 0)
                for b in range(2):
                    pe.wait_ge(up_free[b], freed(AT.up + turned_up, 0) + m2)
                pe.wait_ge(wide_lo_done, AT.wide + i + 3)
                down_unit(AT.down + 24, PAIR_DOWN // 2 * i, 1)

            for f in range(3):
                features(AT.up + f, 0, AT.col + f, f % 2)
            with pe.Fori(0, NPAIR - 1) as i:
                pair(i, False)
            with pe.Fori(NPAIR - 1, NPAIR) as i:
                pair(i, True)
            ffn(F2, 2)


_INS = ['x', 'a_w_in', 'a_ln_g', 'a_ln_b', 'a_w_s', 'a_b_s', 'a_w_out', 'kv_w', 'b_w_q', 'b_w_o', 'rel_table',
        'ffn_w_up', 'ffn_conv_w', 'ffn_conv_b', 'ffn_w_down', 'ln_g', 'ln_b']
_OUT = (1, T, D)


def bucket_pick_constant():
    import numpy as np
    pick = np.zeros((33, len(DIL), TABW), np.float32)
    for g, dil in enumerate(DIL):
        for j in range(TABW):
            delta = 255 - j
            if not 0 <= delta <= 128:
                pick[32, g, j] = 1.0
                continue
            n = delta * dil
            bucket = n
            if n >= 16:
                scaled = np.log(np.float32(n) / np.float32(16)) / np.float32(np.log(2048 / 16)) * np.float32(16)
                bucket = min(16 + int(np.float32(scaled)), 31)
            pick[bucket, g, j] = -1.0
    return pick.reshape(33, len(DIL) * TABW)


def kernel(**inputs):
    import numpy as _np
    import concourse.bacc as _bacc
    from concourse import mybir as _mybir
    from concourse.bass_utils import run_bass_kernel_spmd as _run

    nc = _bacc.Bacc("TRN2", target_bir_lowering=False, num_devices=1)
    arrays, args = {}, []

    def give(name, a):
        arrays[f"in_{name}_dram"] = a
        args.append(nc.dram_tensor(f"in_{name}_dram", a.shape, _mybir.dt.from_np(a.dtype), kind="ExternalInput").ap())

    for name in _INS:
        give(name, _np.ascontiguousarray(inputs[name]))
    give("bucket_pick", bucket_pick_constant())
    give("identity", _np.eye(P, dtype=_np.float32))
    args.append(nc.dram_tensor("out_0_dram", _OUT, _mybir.dt.float32, kind="ExternalOutput").ap())
    program(nc, *args)
    r = _run(nc, [arrays], core_ids=[0])
    return r.results[0]["out_0_dram"]
```
